# Optimizing a Trainium2 kernel written in Bass

```python
import jax, jax.numpy as jnp
from jax import lax
import numpy as np

D_MODEL = 2048
BATCH = 1
SEQ = 256
DEPTH = 1
DEC_BATCH = 8
DEC_SEQ = 1
PAST_LEN = 2048
PAGE_SIZE = 128

MIX_DIM = D_MODEL
FOX_DIM = MIX_DIM // 2
FOX_HEADS = 8
FOX_HEAD_DIM = FOX_DIM // FOX_HEADS
Q_BLOCK = 128
GLA_DIM = MIX_DIM - FOX_DIM
GLA_HEADS = 4
GLA_KEY_DIM = GLA_DIM // 2
GLA_DK = GLA_KEY_DIM // GLA_HEADS
GLA_DV = GLA_DIM // GLA_HEADS
GLA_GATE_RANK = 16
GLA_TAU = 16.0
GLA_CHUNK = 64
MEM_LEN = 256
X_HEADS = 4
X_HEAD_DIM = 128
X_DIM = X_HEADS * X_HEAD_DIM
FFN_DIM = -(-8 * D_MODEL // (3 * 256)) * 256
RMS_EPS = 1e-6
FORGET_BIAS_INIT = 3.0
IN_SPLITS = (FOX_DIM, FOX_DIM, FOX_DIM, FOX_HEADS, GLA_KEY_DIM, GLA_KEY_DIM, GLA_DIM, GLA_DIM, GLA_GATE_RANK)
N_IN = 3 * FOX_DIM + FOX_HEADS + 2 * GLA_KEY_DIM + 2 * GLA_DIM + GLA_GATE_RANK

kernel_name = 'hymba_fox_gla_memxattn_decode_step'

def rmsnorm(x, g):
    xf = x.astype(jnp.float32)
    y = xf * lax.rsqrt(jnp.mean(xf * xf, axis=-1, keepdims=True) + RMS_EPS)
    return (y * g.astype(jnp.float32)).astype(x.dtype)

def mixer_inputs(h, w_in, b_f, w_g2, b_g):
    B, T, _ = h.shape
    z = h @ w_in
    idx = np.cumsum(IN_SPLITS)[:-1].tolist()
    fq, fk, fv, ff, gq, gk, gv, gr, gg = jnp.split(z, idx, axis=-1)
    fox_q = fq.reshape(B, T, FOX_HEADS, FOX_HEAD_DIM)
    fox_k = fk.reshape(B, T, FOX_HEADS, FOX_HEAD_DIM)
    fox_v = fv.reshape(B, T, FOX_HEADS, FOX_HEAD_DIM)
    fox_logf = jax.nn.log_sigmoid((ff + b_f).astype(jnp.float32))
    gla_q = gq.reshape(B, T, GLA_HEADS, GLA_DK) * (GLA_DK ** -0.5)
    gla_k = gk.reshape(B, T, GLA_HEADS, GLA_DK)
    gla_v = gv.reshape(B, T, GLA_HEADS, GLA_DV)
    gla_r = gr.reshape(B, T, GLA_HEADS, GLA_DV)
    gla_logalpha = (jax.nn.log_sigmoid((gg @ w_g2 + b_g).astype(jnp.float32)) / GLA_TAU).reshape(B, T, GLA_HEADS, GLA_DK)
    return fox_q, fox_k, fox_v, fox_logf, gla_q, gla_k, gla_v, gla_r, gla_logalpha

def fox_prompt(q, k, v, logf):
    B, S, H, dh = q.shape
    dT = jnp.cumsum(logf.astype(jnp.float32), axis=1).transpose(0, 2, 1)
    kpos = jnp.arange(S)
    scale = dh ** -0.5

    def block(i):
        start = i * Q_BLOCK
        qb = lax.dynamic_slice_in_dim(q, start, Q_BLOCK, axis=1)
        db = lax.dynamic_slice_in_dim(dT, start, Q_BLOCK, axis=2)
        s = jnp.einsum('bqhd,bkhd->bhqk', qb, k, preferred_element_type=jnp.float32) * scale
        s = s + (db[..., None] - dT[:, :, None, :])
        qpos = start + jnp.arange(Q_BLOCK)
        s = jnp.where(kpos[None, :] <= qpos[:, None], s, -jnp.inf)
        p = jax.nn.softmax(s, axis=-1).astype(v.dtype)
        return jnp.einsum('bhqk,bkhd->bqhd', p, v)

    out = lax.map(block, jnp.arange(S // Q_BLOCK))
    return out.swapaxes(0, 1).reshape(B, S, H, dh)

def fox_sample(q, k_new, v_new, logf_new, k_past, v_past, logf_past):
    dh = q.shape[-1]
    T = q.shape[1]
    P = k_past.shape[1]
    scale = dh ** -0.5
    c_past = jnp.cumsum(logf_past.astype(jnp.float32), axis=1)
    tail = c_past[:, -1:] - c_past
    c_new = jnp.cumsum(logf_new.astype(jnp.float32), axis=1)
    cq = c_new.transpose(0, 2, 1)
    s_past = jnp.einsum('bthd,bshd->bhts', q, k_past, preferred_element_type=jnp.float32) * scale
    s_past = s_past + cq[..., None] + tail.transpose(0, 2, 1)[:, :, None, :]
    s_new = jnp.einsum('bthd,bshd->bhts', q, k_new, preferred_element_type=jnp.float32) * scale
    s_new = s_new + cq[..., None] - cq[:, :, None, :]
    causal = jnp.tril(jnp.ones((T, T), dtype=bool))
    s_new = jnp.where(causal, s_new, -jnp.inf)
    p = jax.nn.softmax(jnp.concatenate([s_past, s_new], axis=-1), axis=-1).astype(v_new.dtype)
    return (jnp.einsum('bhts,bshd->bthd', p[..., :P], v_past)
            + jnp.einsum('bhts,bshd->bthd', p[..., P:], v_new))

def gla_chunk(S0, q, k, v, g):
    q, k, v, g = (a.astype(jnp.float32) for a in (q, k, v, g))
    C = q.shape[1]
    b = jnp.cumsum(g, axis=1)
    causal = jnp.tril(jnp.ones((C, C), dtype=bool))
    diff = b[:, :, None] - b[:, None, :]
    decay = jnp.exp(jnp.where(causal[None, :, :, None, None], diff, -jnp.inf))
    A = jnp.sum(q[:, :, None] * k[:, None] * decay, axis=-1)
    o = (jnp.einsum('btsh,bshv->bthv', A, v)
         + jnp.einsum('bthd,bhdv->bthv', q * jnp.exp(b), S0))
    b_last = b[:, -1]
    S_new = (jnp.exp(b_last)[..., None] * S0
             + jnp.einsum('bshd,bshv->bhdv', k * jnp.exp(b_last[:, None] - b), v))
    return S_new, o

def gla_prompt(q, k, v, g):
    B, S, H, DK = q.shape
    nc = S // GLA_CHUNK

    def to_chunks(a):
        return a.reshape(B, nc, GLA_CHUNK, *a.shape[2:]).swapaxes(0, 1)

    S0 = jnp.zeros((B, H, DK, v.shape[-1]), jnp.float32)

    def step(S_, xs):
        return gla_chunk(S_, *xs)

    S_fin, o = lax.scan(step, S0, (to_chunks(q), to_chunks(k), to_chunks(v), to_chunks(g)))
    return S_fin, o.swapaxes(0, 1).reshape(B, S, H, v.shape[-1])

def mixer_output(o_fox, o_gla, gla_r, g_head, w_out, dtype):
    B, T = o_fox.shape[:2]
    o_g = rmsnorm(o_gla, g_head) * jax.nn.silu(gla_r.astype(jnp.float32))
    cat = jnp.concatenate([o_fox.reshape(B, T, FOX_DIM).astype(dtype),
                           o_g.reshape(B, T, GLA_DIM).astype(dtype)], axis=-1)
    return cat @ w_out

def memory_kv(mem, g_mem, w_k, w_v):
    B, M, _ = mem.shape
    m = rmsnorm(mem, g_mem)
    return (m @ w_k).reshape(B, M, X_HEADS, X_HEAD_DIM), (m @ w_v).reshape(B, M, X_HEADS, X_HEAD_DIM)

def cross_attn(h, mk, mv, w_q, w_o):
    B, T, _ = h.shape
    q = (h @ w_q).reshape(B, T, X_HEADS, X_HEAD_DIM)
    s = jnp.einsum('bthd,bmhd->bhtm', q, mk, preferred_element_type=jnp.float32) * (X_HEAD_DIM ** -0.5)
    p = jax.nn.softmax(s, axis=-1).astype(mv.dtype)
    o = jnp.einsum('bhtm,bmhd->bthd', p, mv).reshape(B, T, X_DIM)
    return o @ w_o

def swiglu(h, w_gate, w_up, w_down):
    return (jax.nn.silu(h @ w_gate) * (h @ w_up)) @ w_down

def setup_inputs(seed: int = 0) -> dict:
    key = jax.random.key(seed)
    ks = iter(jax.random.split(key, 40))

    def nrm(shape, scale):
        return jax.random.normal(next(ks), shape, jnp.float32) * scale

    def gain(shape):
        return 1.0 + nrm(shape, 0.02)

    n_pages = PAST_LEN // PAGE_SIZE
    n_used = DEC_BATCH * n_pages
    n_pool = (5 * n_used + 3) // 4
    x_prompt = nrm((BATCH, SEQ, D_MODEL), 1.0)
    x_sample = nrm((DEC_BATCH, DEC_SEQ, D_MODEL), 1.0)
    mem_prompt = nrm((BATCH, MEM_LEN, D_MODEL), 1.0)
    cache_fox_k = nrm((DEPTH, n_pool, PAGE_SIZE, FOX_HEADS, FOX_HEAD_DIM), 1.0)
    cache_fox_v = nrm((DEPTH, n_pool, PAGE_SIZE, FOX_HEADS, FOX_HEAD_DIM), 1.0)
    cache_fox_logf = jax.nn.log_sigmoid(FORGET_BIAS_INIT + nrm((DEPTH, n_pool, PAGE_SIZE, FOX_HEADS), 1.0))
    state_gla = nrm((DEPTH, DEC_BATCH, GLA_HEADS, GLA_DK, GLA_DV), 1.0)
    cache_mem_k = nrm((DEPTH, DEC_BATCH, MEM_LEN, X_HEADS, X_HEAD_DIM), 1.0)
    cache_mem_v = nrm((DEPTH, DEC_BATCH, MEM_LEN, X_HEADS, X_HEAD_DIM), 1.0)
    page_table = jax.random.permutation(next(ks), n_pool)[:n_used].reshape(DEC_BATCH, n_pages).astype(jnp.int32)
    return {
        'x_prompt': x_prompt,
        'x_sample': x_sample,
        'mem_prompt': mem_prompt,
        'cache_fox_k': cache_fox_k,
        'cache_fox_v': cache_fox_v,
        'cache_fox_logf': cache_fox_logf,
        'state_gla': state_gla,
        'cache_mem_k': cache_mem_k,
        'cache_mem_v': cache_mem_v,
        'page_table': page_table,
        'g_mix': gain((DEPTH, D_MODEL)),
        'w_in': nrm((DEPTH, D_MODEL, N_IN), D_MODEL ** -0.5),
        'b_forget': FORGET_BIAS_INIT + nrm((DEPTH, FOX_HEADS), 0.1),
        'w_gla_gate': nrm((DEPTH, GLA_GATE_RANK, GLA_KEY_DIM), GLA_GATE_RANK ** -0.5),
        'b_gla_gate': nrm((DEPTH, GLA_KEY_DIM), 0.01),
        'g_gla_head': gain((DEPTH, GLA_DV)),
        'w_out': nrm((DEPTH, MIX_DIM, D_MODEL), MIX_DIM ** -0.5),
        'g_cross': gain((DEPTH, D_MODEL)),
        'g_mem': gain((DEPTH, D_MODEL)),
        'w_xq': nrm((DEPTH, D_MODEL, X_DIM), D_MODEL ** -0.5),
        'w_xk': nrm((DEPTH, D_MODEL, X_DIM), D_MODEL ** -0.5),
        'w_xv': nrm((DEPTH, D_MODEL, X_DIM), D_MODEL ** -0.5),
        'w_xo': nrm((DEPTH, X_DIM, D_MODEL), X_DIM ** -0.5),
        'g_ffn': gain((DEPTH, D_MODEL)),
        'w_ffn_gate': nrm((DEPTH, D_MODEL, FFN_DIM), D_MODEL ** -0.5),
        'w_ffn_up': nrm((DEPTH, D_MODEL, FFN_DIM), D_MODEL ** -0.5),
        'w_ffn_down': nrm((DEPTH, FFN_DIM, D_MODEL), FFN_DIM ** -0.5),
        'g_final': gain((D_MODEL,)),
    }

def reference(x_prompt, x_sample, mem_prompt, cache_fox_k, cache_fox_v, cache_fox_logf, state_gla,
              cache_mem_k, cache_mem_v, page_table, g_mix, w_in, b_forget, w_gla_gate, b_gla_gate,
              g_gla_head, w_out, g_cross, g_mem, w_xq, w_xk, w_xv, w_xo, g_ffn, w_ffn_gate, w_ffn_up,
              w_ffn_down, g_final):
    xp = x_prompt
    xs = x_sample
    Bs = x_sample.shape[0]
    past = page_table.shape[1] * cache_fox_k.shape[2]
    pk, pv, pf, pS, pmk, pmv = [], [], [], [], [], []
    sk, sv, sf, sS = [], [], [], []
    for l in range(DEPTH):
        h = rmsnorm(xp, g_mix[l])
        fq, fk, fv, flogf, gq, gk, gv, gr, glog = mixer_inputs(h, w_in[l], b_forget[l], w_gla_gate[l], b_gla_gate[l])
        o_f = fox_prompt(fq, fk, fv, flogf)
        S_fin, o_g = gla_prompt(gq, gk, gv, glog)
        xp = xp + mixer_output(o_f, o_g, gr, g_gla_head[l], w_out[l], xp.dtype)
        mk, mv = memory_kv(mem_prompt, g_mem[l], w_xk[l], w_xv[l])
        xp = xp + cross_attn(rmsnorm(xp, g_cross[l]), mk, mv, w_xq[l], w_xo[l])
        xp = xp + swiglu(rmsnorm(xp, g_ffn[l]), w_ffn_gate[l], w_ffn_up[l], w_ffn_down[l])
        pk.append(fk); pv.append(fv); pf.append(flogf); pS.append(S_fin); pmk.append(mk); pmv.append(mv)

        h = rmsnorm(xs, g_mix[l])
        fq, fk, fv, flogf, gq, gk, gv, gr, glog = mixer_inputs(h, w_in[l], b_forget[l], w_gla_gate[l], b_gla_gate[l])
        k_past = cache_fox_k[l, page_table].reshape(Bs, past, FOX_HEADS, FOX_HEAD_DIM)
        v_past = cache_fox_v[l, page_table].reshape(Bs, past, FOX_HEADS, FOX_HEAD_DIM)
        f_past = cache_fox_logf[l, page_table].reshape(Bs, past, FOX_HEADS)
        o_f = fox_sample(fq, fk, fv, flogf, k_past, v_past, f_past)
        S_new, o_g = gla_chunk(state_gla[l].astype(jnp.float32), gq, gk, gv, glog)
        xs = xs + mixer_output(o_f, o_g, gr, g_gla_head[l], w_out[l], xs.dtype)
        xs = xs + cross_attn(rmsnorm(xs, g_cross[l]), cache_mem_k[l], cache_mem_v[l], w_xq[l], w_xo[l])
        xs = xs + swiglu(rmsnorm(xs, g_ffn[l]), w_ffn_gate[l], w_ffn_up[l], w_ffn_down[l])
        sk.append(fk); sv.append(fv); sf.append(flogf); sS.append(S_new)

    y_prompt = rmsnorm(xp, g_final)
    y_sample = rmsnorm(xs, g_final)
    return (y_prompt, y_sample,
            jnp.stack(pk), jnp.stack(pv), jnp.stack(pf), jnp.stack(pS), jnp.stack(pmk), jnp.stack(pmv),
            jnp.stack(sk), jnp.stack(sv), jnp.stack(sf), jnp.stack(sS))


_drawn_inputs = setup_inputs


def setup_inputs(seed=0):
    import zlib

    import numpy as np

    out = dict(_drawn_inputs(seed))
    spreads = {}
    factors = {'b_gla_gate': 8.0,
     'g_gla_head': 7.107,
     'g_cross': 8.0,
     'g_mem': 2.833,
     'g_ffn': 4.24,
     'g_final': 7.968,
     'cache_fox_logf': 3.417}
    for name, (base, spread) in spreads.items():
        noise = np.random.default_rng([zlib.crc32(name.encode()), seed]).standard_normal(out[name].shape)
        drawn = base * np.exp(spread * noise) if base else spread * noise
        out[name] = __import__('jax').numpy.asarray(drawn.astype(out[name].dtype))
    for name, factor in factors.items():
        out[name] = (out[name] * factor).astype(out[name].dtype)
    return out
```

```python
from contextlib import ExitStack

import numpy as np
import concourse.bass as bass
from concourse import mybir
from concourse.alu_op_type import AluOpType as ALU

P = 128
D = 2048
NP_ = 256
ND = 8
T = NP_ + ND
C = D // P
H = 8
PAGES = 16
PAGE = 128
GH = 4
DV = 256
XH = 4
MEM = 256
FFN = 5632
HALF = FFN // P // 2
SUB = HALF // 2
RANK = 16
LEVELS = 6
EPS = 1e-6
SCALE = float(P) ** -0.5
NARROW = 40

SLOTS = 8
MIX = [("k", j) for j in range(8)] + [x for j in range(8) for x in (("v", 2 * j), ("v", 2 * j + 1), ("k", 8 + j))]

K_ID, K_ONE, K_CAUS, K_SEL, K_SCAN = 0, P, 2 * P, 3 * P, 3 * P + 16
K_ALL = K_SCAN + NP_


def constants():
    k = np.zeros((P, K_ALL), np.float32)
    r = np.arange(P)
    k[:, K_ID:K_ID + P] = np.eye(P)
    k[:, K_ONE:K_ONE + P] = 1.0
    k[:, K_CAUS:K_CAUS + P] = np.where(r[None, :] <= r[:, None], 0.0, -1e30)
    for g in range(4):
        k[32 * g + 2 * g, K_SEL + g] = 1.0
        k[32 * g + 2 * g + 1, K_SEL + 4 + g] = 1.0
        k[32 * g + g, K_SEL + 8 + g] = 1.0
    k[:, K_SCAN:K_SCAN + NP_] = (np.arange(NP_) % 64 != 0)[None, :]
    s, t = r[:, None], r[None, :]
    masks = np.zeros((P, LEVELS + 1, P), np.uint8)
    for l in range(LEVELS):
        b = 2 << l
        masks[:, l] = (s // b == t // b) & (s % b < b // 2) & (t % b >= b // 2)
    masks[:, LEVELS] = s == t
    later = np.zeros((P, 2, P), np.float32)
    later[:, 0] = s > t
    later[:, 1] = (s // PAGES == t // PAGES) & (s % PAGES > t % PAGES)
    return k, later.reshape(P, 2 * P), masks.reshape(P, -1).view(np.int32)


ST = {}


def _stages():
    n = 0
    for name, count, blocks in (("fox", 24, C), ("gla", 24, C), ("mem", 8, C), ("out", 16, C), ("xq", 4, C), ("xo", 16, 4),
                                ("gu0", 2 * HALF, C), ("dn0", 32, SUB), ("gu1", 2 * HALF, C), ("dn1", 32, SUB)):
        ST[name] = (n, count, blocks)
        n += count
    return n


N_PANELS = _stages()
ORDER = list(ST)


def acc_count():
    out, a = {}, 0
    for name in ORDER:
        out[name] = a
        a += ST[name][1] // (2 if name.startswith("dn") else 1)
    return out


ACC = acc_count()


def build(nc, io):
    f32, f32r, i32 = mybir.dt.float32, mybir.dt.float32r, mybir.dt.int32
    ACT = mybir.ActivationFunctionType
    AX = mybir.AxisListType
    ds = bass.ds

    base = (nc.sbuf_base + 63) // 64 * 64

    def at(name, off, shape, dt=f32):
        return nc.alloc_sbuf_tensor_at(name, [shape[0], int(np.prod(shape[1:]))], dt, offset=base + off)

    def view(t, *dims):
        names = "abcd"[:len(dims)]
        if len(dims) == 1:
            return t[:, :]
        return t[:, :].rearrange(f"p ({' '.join(names)}) -> p {' '.join(names)}", **{n: d for n, d in zip(names, dims)})

    A0 = 0
    B0 = A0 + C * T * 4
    C0 = B0 + 2 * C * T * 4
    D0 = C0 + 48 * T * 4
    E0 = D0 + 6 * C * P * 4
    F0 = E0 + SLOTS * 1024 * 4
    G0 = F0 + 2 * XH * MEM * 4
    H0 = G0 + 2 * 4 * T * 4 + T * 4
    TW = T * 4

    x_res = view(at("x_res", A0, [P, C, T]), C, T)
    hh = view(at("hh", B0, [P, C, T], f32r), C, T)
    hl = view(at("hl", B0 + C * TW, [P, C, T], f32r), C, T)
    z = view(at("z", C0, [P, 48, T]), 48, T)
    raw = view(at("raw", D0, [P, 4, C * P]), 4, C * P)
    whi = view(at("whi", D0 + 4 * C * P * 4, [P, 2, C * P], f32r), 2, C * P)
    wlo = view(at("wlo", D0, [P, 4, C * P], f32r), 4, C * P)
    page = view(at("page", E0, [P, SLOTS, 1024]), SLOTS, 1024)
    mkv = view(at("mkv", F0, [P, 2 * XH, MEM]), 2 * XH, MEM)
    nb = view(at("nb", G0, [P, 2, 4, T]), 2, 4, T)
    rstd = at("rstd", G0 + 8 * TW, [P, T])
    o = H0

    def keep(name, *dims, parts=P, dt=f32):
        nonlocal o
        t = at(name, o, [parts, *dims], dt)
        o += (int(np.prod(dims)) * 4 + 31) // 32 * 32
        return t
    kst = keep("kst", K_ALL)
    masks4 = keep("masks", (LEVELS + 1) * P // 4, dt=i32)
    masks = masks4[:, :].bitcast(mybir.dt.uint8)
    gains = view(keep("gains", 5, C), 5, C)
    small = keep("small", 8)
    g_log = view(keep("g_log", GH, T), GH, T)
    logf = keep("logf", T, parts=ND)
    ndq = keep("ndq", NP_, parts=ND)
    pts = keep("pts", P, parts=1, dt=i32)
    ptc = keep("ptc", 1, dt=i32)
    snew = view(keep("snew", H, ND), H, ND)
    ofd = view(keep("ofd", H, ND), H, ND)
    sm8 = keep("sm8", 64)
    assert base + o <= nc.sbuf_usable_end, (base + o, nc.sbuf_usable_end)
    ident, ones = kst[:, K_ID:K_ID + P], kst[:, K_ONE:K_ONE + P]
    causal = kst[:, K_CAUS:K_CAUS + P]

    qd = at("qd", A0, [P, 1024])
    qb = at("qb", A0 + 4096, [P, 1024])
    tail = at("tail", A0 + 8192, [P, 1024])
    prob = view(at("prob", A0 + 12288, [P, PAGES, 32]), PAGES, 32)
    s_raw = view(at("s_raw", A0 + 14336, [P, PAGES, H]), PAGES, H)
    s_bias = view(at("s_bias", A0 + 14848, [P, PAGES, H]), PAGES, H)
    osb = at("osb", A0 + 15360, [P, 256])
    g_ofd = view(at("g_ofd", A0 + 16384, [P, 8, ND]), 8, ND)
    g_eg = view(at("g_eg", A0 + 16640, [P, GH, ND]), GH, ND)
    f_nat = at("f_nat", F0, [P, 1024])
    t_sb = at("t_sb", F0 + 4096, [P, 1024])
    r_sb = at("r_sb", G0, [P, 1024])
    lf_in = view(at("lf_in", G0 + 4096, [ND, H, ND]), H, ND)
    sq_in = view(at("sq_in", G0 + 4608, [P, H, ND]), H, ND)
    lfb = view(at("lfb", G0 + 7232, [P, H, ND]), H, ND)
    lf_t = view(at("lf_t", G0 + 5120, [ND, 2, T]), 2, T)
    later = at("later", C0 + 47 * TW, [P, 256])
    wgate = at("wgate", C0 + 36 * TW, [RANK, 4 * P])
    ggs = at("ggs", G0, [RANK, T])
    n_raw = at("n_raw", C0 + 41 * TW, [P, C * NARROW])
    n_hi = at("n_hi", C0 + 44 * TW, [P, C * NARROW], f32r)
    n_lo = at("n_lo", C0 + 38 * TW, [P, C * NARROW], f32r)
    assert C * NARROW * 4 <= 3 * TW
    a_q = at("a_q", G0, [P, 256])
    a_v = at("a_v", G0 + 1024, [P, 256])
    a_vn = view(at("a_vn", G0 + 2048, [P, 2, P]), 2, P)
    a_s = view(at("a_s", G0 + 3072, [P, 2, 256]), 2, 256)
    a_pt = view(at("a_pt", G0 + 5120, [P, 2, 256]), 2, 256)
    a_o = at("a_o", G0 + 7168, [P, 256])
    a_nd = at("a_nd", G0 + 8192, [ND, 256])
    o_d = 0

    def in_ring(name, *dims):
        nonlocal o_d
        t = at(name, D0 + o_d, [P, *dims])
        o_d += (int(np.prod(dims)) * 4 + 31) // 32 * 32
        assert o_d <= 6 * C * P * 4
        return view(t, *dims)
    g_v, g_vn, g_kn, g_at = in_ring("g_v", 2, 256), in_ring("g_vn", 2, 256), in_ring("g_kn", 2, P), in_ring("g_at", 2, P)
    g_st = in_ring("g_st", 4, 256)
    g_b, g_q, g_k = in_ring("g_b", 256), in_ring("g_q", 256), in_ring("g_k", 256)
    g_eb, g_ke, g_qe = in_ring("g_eb", 256), in_ring("g_ke", 256), in_ring("g_qe", 256)
    g_d = in_ring("g_d", LEVELS + 1, 256)
    g_dd = in_ring("g_dd", 1024)
    g_s = in_ring("g_s", 2, 1024)
    g_cols = in_ring("g_cols", 2, 3, GH)
    g_t = view(at("g_t", C0 + 24 * TW, [P, 3, GH, T]), 3, GH, T)
    g_n = view(at("g_n", C0, [P, 3, 2, T]), 3, 2, T)
    f_hi = view(at("f_hi", C0, [P, HALF, T], f32r), HALF, T)
    f_lo = view(at("f_lo", C0 + HALF * TW, [P, HALF, T], f32r), HALF, T)
    f_sg = at("f_sg", G0, [P, T])
    f_h = view(at("f_h", G0 + TW, [P, 2, T]), 2, T)
    x_q = view(at("x_q", C0, [P, XH, T]), XH, T)
    x_qd = at("x_qd", C0 + 4 * TW, [P, 512])
    x_qb = view(at("x_qb", C0 + 6 * TW, [P, 2, 512]), 2, 512)
    x_s = view(at("x_s", C0 + 10 * TW, [P, ND, 2, XH]), ND, 2, XH)
    x_p = view(at("x_p", C0 + 11 * TW, [P, ND, 2, 32]), ND, 2, 32)
    x_o = at("x_o", C0 + 13 * TW, [P, 256])
    x_sm = at("x_sm", C0 + 14 * TW, [P, 256])
    x_od = view(at("x_od", C0 + 15 * TW, [P, XH, ND]), XH, ND)

    ctx = ExitStack()
    with ctx:
        bank = [ctx.enter_context(nc.psum_tensor(f"bank{i}", [P, 512], f32)) for i in range(8)]
        sems = {}
        PARAMS = 16 * 7

        def S(name):
            if name not in sems:
                sems[name] = ctx.enter_context(nc.semaphore(name))
            return sems[name]

        block = ctx.enter_context(nc.Block())

        def wait_apart(eng, sem, value):
            eng.wait_ge(S("params_in"), PARAMS)
            eng.wait_ge(S(sem), value)

        class Chain:
            def __init__(self, eng, name):
                self.eng, self.sem, self.start, self.n = eng, S(name), 0, 0

            def link(self, ins):
                self.n += 1
                ins.then_inc(self.sem, 1)
                self.eng.wait_ge(self.sem, self.start + self.n)

            def turn(self, first, i, per_turn):
                self.start, self.n = first + i * per_turn, 0

            def after(self, first, turns, per_turn):
                assert self.n == per_turn, (self.n, per_turn)
                self.start, self.n = first + turns * per_turn, 0

            @property
            def count(self):
                return self.start + self.n


        @block.sync
        def _(sp):
            for dst, src in ((gains.rearrange("p a b -> p (a b)"), "gains"), (kst[:, :], "kst"), (masks4[:, :], "masks"), (small[:, :], "small"), (wgate[:, :], "wgate"),
                             (later[:, :], "later"), (n_raw[:, :], "w_narrow")):
                sp.dma_start(dst, io[src]).then_inc(S("params_in"), 16)
            x_fm = io["x_fm"].rearrange("p (a b) -> p a b", a=C)
            mem_fm = io["mem_fm"].rearrange("p (a b) -> p a b", a=C)

            def stream(src, n, m):
                for g in range(8):
                    if g < 2 and m:
                        sp.wait_ge(S("n_lo_done"), 4 * m)
                    elif 2 <= g < 6:
                        sp.wait_ge(S("n_ss"), 4 * m + min(g - 1, 4))
                    elif g >= 6:
                        sp.wait_ge(S("n_lo_done"), 4 * m + g - 5)
                    sp.dma_start(nb[:, g % 2, :, 0:n], src[:, 4 * (g % 4):4 * (g % 4) + 4, :]).then_inc(S(f"nb_in{g % 2}"), 16)

            def load(name, i, k):
                first, count, blocks = ST[name]
                if not (first == 0 and isinstance(i, int) and i == 0):
                    sp.wait_ge(S("mm_done"), first + 4 * i + k - 3)
                sp.dma_start(raw[:, k, 0:blocks * P], io["p_" + name][ds((4 * i + k) * P, P), :]).then_inc(S(f"w_in{k}"), 16)

            def loads(name, lo=0):
                with sp.Fori(lo, ST[name][1] // 4) as i:
                    for k in range(4):
                        load(name, i, k)

            stream(x_fm, T, 0)
            for k in range(4):
                load("fox", 0, k)
            loads("fox", 1)
            loads("gla")
            for k in range(4):
                load("mem", 0, k)
            sp.wait_ge(S("tail_ready"), 1)
            stream(mem_fm, MEM, 1)
            for k in range(4):
                load("mem", 1, k)
            sp.wait_ge(S("gla_done"), 1)
            for k in range(4):
                load("out", 0, k)
            sp.dma_start(x_res, x_fm).then_inc(S("x_in"), 16)
            loads("out", 1)
            for k in range(4):
                load("xq", 0, k)
            for name in ORDER[5:]:
                loads(name)
            sp.wait_ge(S("y_done"), 4)
            sp.dma_start(io["o_y"], x_res.rearrange("p a b -> p (a b)")).then_inc(S("y_out"), 16)
            sp.wait_ge(S("y_out"), 16)

        @block.gpsimd
        def _(pool):
            pool.dma_start(pts[:, :], io["pt_row"]).then_inc(S("pt_in"), 16)
            pool.dma_start(ptc[:, :], io["pt_col"]).then_inc(S("pt_in"), 16)
            pool.wait_ge(S("pt_in"), 32)
            pool.indirect_dma_start(f_nat[:, :], None, io["lf"], bass.IndirectOffsetOnAxis(ap=ptc[:, 0:1], axis=0)
                                    ).then_inc(S("lf_in"), 16)

            def fetch(src, index, slot, sem=None, value=0):
                r = pool.value_load(pts[0:1, ds(index, 1)], min_val=0, max_val=io["n_pool"] - 1)
                if sem:
                    pool.wait_ge(S(sem), value)
                pool.dma_start(page[:, slot, :], io[src][ds(r * P, P), :]).then_inc(S(f"page_in{slot}"), 16)

            for j in range(8):
                fetch("kc", j, j)
            for j in range(8, 16):
                fetch("kc", j, j - 8, "k_used", j - 7)

            def mixed(t, q):
                if q >= SLOTS:
                    kind, j, turn = *MIX[q - SLOTS], t
                elif isinstance(t, int):
                    kind, j, turn = "k", 16 - SLOTS + q, 0
                else:
                    kind, j, turn = *MIX[q + 32 - SLOTS], t - 1
                sem, value = ("k_used", 16 * turn + j + 1) if kind == "k" else ("v_used", 16 * turn - 15 + j)
                now, j = MIX[q]
                fetch("kc" if now == "k" else "vc", 16 * t + j if now == "k" else 16 * t - 16 + j, q % SLOTS, sem, value)

            for q in range(32):
                mixed(1, q)
            with pool.Fori(2, 8) as t:
                for q in range(32):
                    mixed(t, q)
            for j in range(16):
                if j < SLOTS:
                    kind, i = MIX[32 - SLOTS + j]
                    fetch("vc", 112 + j, j, *(("k_used", 113 + i) if kind == "k" else ("v_used", 97 + i)))
                else:
                    fetch("vc", 112 + j, j - SLOTS, "v_used", 113 + j - SLOTS)
            ck = io["cmk"].rearrange("(b m p) n -> b p m n", p=P, m=2)
            cv = io["cmv"].rearrange("(b m p) n -> b p m n", p=P, m=2)
            for b in range(16):
                if b < 8:
                    pool.wait_ge(S("v_used"), 121 + b)
                else:
                    pool.wait_ge(S("xk_used"), b - 7)
                pool.dma_start(page[:, b % 8, :].rearrange("p (m n) -> p m n", m=2), (ck if b < 8 else cv)[b % 8]
                               ).then_inc(S(f"page_in{b % 8}"), 16)

        def arrived(t, q):
            return 16 * (q // 8 + 1) if isinstance(t, int) and t == 0 else 64 * t - 32 + 16 * (q // 8 + 1)

        def flat(ap):
            return ap.rearrange("p a b -> p (a b)")

        def row(ap):
            return ap.rearrange("p (a b) -> p a b", a=1)

        def colv(ap):
            return ap.rearrange("p (a b) -> p a b", b=1)

        def blocks_after(name):
            p = ORDER.index(name) + 1
            return ST[ORDER[p]][2] if p < len(ORDER) else 0

        def some_panels(eng, lo, hi, step):
            with eng.Fori(lo, hi) as i:
                for k in range(4):
                    step(i, k, C)

        def for_panels(eng, ch, name, step, links=0):
            first, count, blocks = ST[name]
            nxt, links0 = blocks_after(name), ch.count
            if count > 4:
                with eng.Fori(0, count // 4 - 1) as i:
                    ch.turn(links0, i, links)
                    for k in range(4):
                        step(i, k, blocks)
                ch.after(links0, count // 4 - 1, links)
            for k in range(4):
                step(count // 4 - 1, k, blocks if k < 2 else nxt)

        @block.scalar
        def _(act):
            ch = Chain(act, "act_chain")

            def cast(first, i, k, blocks):
                kk, ii = k % 4, i + k // 4
                act.wait_ge(S(f"w_in{kk}"), 16 * (ii + first // 4 + 1))
                act.activation(whi[:, kk % 2, 0:blocks * P], raw[:, kk, 0:blocks * P], ACT.Copy).then_inc(S("w_hi"), 1)

            def step(name, i, k, blocks):
                first = ST[name][0]
                act.wait_ge(S("mm_done"), first + 4 * i + k + 1)
                if blocks:
                    cast(first, i, k + 2, blocks)

            def casts(name):
                for_panels(act, ch, name, lambda i, k, b: step(name, i, k, b))

            def norm(m, n, col, streamed, final=False):
                for g in range(4):
                    if streamed:
                        act.wait_ge(S(f"nb_in{g % 2}"), 16 * (4 * m + g // 2 + 1))
                        src = nb[:, g % 2, :, 0:n]
                    else:
                        src = x_res[:, 4 * g:4 * g + 4, :]
                        if g < 2:
                            act.wait_ge(S("n_go"), m - 1)
                        else:
                            act.wait_ge(S("n_ss"), 4 * m + g - 1)
                    act.activation(nb[:, g % 2, :, 0:n], src, ACT.Square).then_inc(S("n_sq"), 1)
                act.wait_ge(S("n_ss"), 4 * m + 4)
                act.activation(rstd[:, 0:n], bank[6][:, 0:n], ACT.Sqrt, bias=small[:, 7:8], scale=1.0 / D).then_inc(S("n_sqrt"), 1)
                for g in range(0 if final else 4):
                    act.wait_ge(S("n_xn"), 4 * m + g + 1)
                    for c in range(4):
                        ins = act.activation(hh[:, 4 * g + c, 0:n], nb[:, g % 2, c, 0:n], ACT.Copy,
                                             scale=gains[:, col, 4 * g + c:4 * g + c + 1])
                    ins.then_inc(S("n_hi"), 1)

            act.sem_inc(S("g_o"), 1)
            for name in ("st_out0", "st_out1", "stp_out"):
                act.sem_inc(S(name), 16)
            act.wait_ge(S("params_in"), PARAMS)
            act.activation(n_hi[:, :], n_raw[:, :], ACT.Copy).then_inc(S("nw_hi"), 1)
            norm(0, T, 0, True)
            act.wait_ge(S("lf_neg"), 1)
            ch.link(act.activation(lf_t[:, 1, :], lf_t[:, 1, :], ACT.Exp))
            act.activation(lf_t[:, 1, :], lf_t[:, 1, :], ACT.Ln, bias=ones[0:ND, 0:1]).then_inc(S("lf_ln"), 1)
            cast(0, 0, 0, C)
            cast(0, 0, 1, C)
            def fox_step(i, k, b):
                step("fox", i, k, b)

            def q_copy(t):
                act.wait_ge(S("q_ps"), t + 1)
                if not (isinstance(t, int) and t == 0):
                    act.wait_ge(S("k_used"), 16 * t)
                for n in range(2):
                    ins = act.activation(qb[:, 512 * n:512 * n + 512], bank[2 + n][:, :], ACT.Copy, scale=SCALE)
                ins.then_inc(S("q_b"), 1)

            some_panels(act, 0, 2, fox_step)
            act.wait_ge(S("gg_neg"), 1)
            ch.link(act.activation(g_t[:, 1, :, :], g_t[:, 1, :, :], ACT.Exp))
            act.activation(g_t[:, 1, :, :], g_t[:, 1, :, :], ACT.Ln, bias=ones[:, 0:1]).then_inc(S("gg_ln"), 1)
            act.wait_ge(S("gates_done"), 1)
            act.activation(g_eg, g_log[:, :, NP_:T], ACT.Exp).then_inc(S("g_eg"), 1)
            q_copy(0)
            for i in range(2, 6):
                for k in range(4):
                    fox_step(i, k, C)
                if i == 2:
                    act.wait_ge(S("t_ps"), 1)
                    for n in range(2):
                        ins = act.activation(t_sb[:, 512 * n:512 * n + 512], bank[2 + n][:, :], ACT.Copy)
                    ins.then_inc(S("t_sb"), 1)
            act.wait_ge(S("z_fox"), 1)
            act.dma_start(io["o_kv"], flat(z[:, 8:24, :])).then_inc(S("out_act"), 16)
            act.dma_start(io["o_logf"], logf[:, :]).then_inc(S("out_act"), 16)

            def exp_scores(t):
                act.wait_ge(S("s_sub"), t)
                act.activation(prob[:, :, 0:H], s_bias, ACT.Exp)
                act.activation(sm8[:, 16:24], sm8[:, 16:24], ACT.Exp).then_inc(S("p_ready"), 1)

            def take_o(t):
                act.wait_ge(S("v_used"), 16 * t)
                act.activation(osb[:, :], bank[4][:, 0:256], ACT.Copy).then_inc(S("o_sb"), 1)

            def panel_turn(t, name, i0):
                def some(lo, hi):
                    for k in range(lo, hi):
                        step(name, i0 + k // 4, k % 4, C)
                q_copy(t)
                some(0, 2)
                exp_scores(t)
                some(2, 7)
                take_o(t)
                some(7, 8)

            with act.Fori(1, 4) as t:
                panel_turn(t, "gla", 2 * t - 2)
            norm(1, MEM, 2, True)
            q_copy(4)
            for k in range(8):
                if k == 2:
                    exp_scores(4)
                if k == 7:
                    take_o(4)
                step("mem", k // 4, k % 4, C if k < 6 else 0)
            act.wait_ge(S("mkv_done"), 1)
            act.dma_start(io["o_mkv"], flat(mkv)).then_inc(S("out_act"), 16)

            def f_stage(n, qsrc, vsrc):
                wait_apart(act, "a_free", n + 1)
                act.activation(a_q[:, :], qsrc, ACT.Copy, scale=SCALE)
                act.activation(a_v[:, :], vsrc, ACT.Copy).then_inc(S("a_staged"), 1)
                act.wait_ge(S("a_vps"), n + 1)
                act.activation(flat(a_vn), bank[7][:, 0:256], ACT.Copy).then_inc(S("a_vn"), 1)

            def f_exp(n):
                act.wait_ge(S("a_max"), n + 1)
                for q in range(2):
                    ins = act.activation(a_s[:, q, :], a_s[:, q, :], ACT.Exp, bias=sm8[:, 50 + q:51 + q],
                                         accum_out=sm8[:, 52 + q:53 + q])
                ins.then_inc(S("a_exp"), 1)

            def f_pt(n):
                act.wait_ge(S("a_ptps"), n + 1)
                act.activation(flat(a_pt), bank[6][:, :], ACT.Copy).then_inc(S("a_pt"), 1)

            def f_out_hi(n, i):
                wait_apart(act, "a_osb", n + 1)
                act.activation(hh[:, ds(i, 1), 0:NP_], row(a_o[:, :]), ACT.Copy).then_inc(S("a_ohi"), 1)

            s_in = io["s0"].rearrange("(b h k) v -> b k h v", h=GH, k=P)
            s_out = io["o_sts"].rearrange("(b h k) v -> b k h v", h=GH, k=P)

            def state_load(i, s):
                act.wait_ge(S("gs_free"), 2 * i + s + 1)
                act.wait_ge(S(f"st_out{s}"), 16 * i + 16)
                act.dma_start(g_s[:, s, :].rearrange("p (h v) -> p h v", h=GH),
                              s_in[ds(2 * i + s, 1), :, :, :].rearrange("a k h v -> k (a h) v")).then_inc(S(f"st_in{s}"), 16)

            def state_decay(i, s):
                act.wait_ge(S("gd_cols"), 2 * i + s + 1)
                act.wait_ge(S(f"st_in{s}"), 16 * (i + 1))
                for h in range(GH):
                    ins = act.activation(g_s[:, s, 256 * h:256 * h + 256], g_s[:, s, 256 * h:256 * h + 256], ACT.Copy,
                                         scale=g_cols[:, s, 2, h:h + 1])
                ins.then_inc(S("gd_dec"), 1)

            def state_store(i, s):
                act.wait_ge(S("gd_new"), 2 * i + s + 1)
                act.dma_start(s_out[ds(2 * i + s, 1), :, :, :].rearrange("a k h v -> k (a h) v"),
                              g_s[:, s, :].rearrange("p (h v) -> p h v", h=GH)).then_inc(S(f"st_out{s}"), 16)

            def head_turn(t, i):
                def fox_args(c):
                    return flat(z[:, ds(2 * i + c, 1), 0:NP_]), flat(z[:, ds(2 * H + 2 * i + c, 1), 0:NP_])
                if not (isinstance(t, int) and t == 8):
                    q_copy(t)
                for s in range(2):
                    state_load(i, s)
                state_decay(i, 0)
                exp_scores(t)
                f_stage(2 * i, *fox_args(0))
                wait_apart(act, "g_free", i + 1)
                act.activation(g_q, flat(z[:, ds(24 + i, 1), 0:NP_]), ACT.Copy, scale=SCALE)
                act.activation(g_k, flat(z[:, ds(28 + i, 1), 0:NP_]), ACT.Copy)
                act.activation(g_v, z[:, ds(32 + 2 * i, 2), 0:NP_], ACT.Copy).then_inc(S("g_staged"), 1)
                act.wait_ge(S("g_diff"), i + 1)
                act.activation(g_eb, g_b, ACT.Exp)
                act.activation(g_d, g_d, ACT.Exp).then_inc(S("g_exp"), 1)
                act.wait_ge(S("g_vps"), i + 1)
                act.activation(flat(g_vn), bank[0][:, :], ACT.Copy).then_inc(S("g_vn"), 1)
                f_exp(2 * i)
                state_store(i, 0)
                state_decay(i, 1)
                act.wait_ge(S("g_kps"), i + 1)
                act.activation(flat(g_kn), bank[1][:, 0:256], ACT.Copy).then_inc(S("g_kn"), 1)
                f_pt(2 * i)
                state_store(i, 1)
                f_out_hi(2 * i, 2 * i)
                f_stage(2 * i + 1, *fox_args(1))
                act.wait_ge(S("g_state"), i + 1)
                act.dma_start(io["o_stp"][ds(i * P, P), :], g_st[:, 3, :]).then_inc(S("stp_out"), 16)
                wait_apart(act, "g_ops", i + 1)
                act.activation(z[:, ds(32 + 2 * i, 2), 0:NP_], bank[0][:, :].rearrange("p (a b) -> p a b", a=2), ACT.Copy
                               ).then_inc(S("g_o"), 1)
                f_exp(2 * i + 1)
                f_pt(2 * i + 1)
                take_o(t)
                f_out_hi(2 * i + 1, 2 * i + 1)

            with act.Fori(5, 8) as t:
                head_turn(t, t - 5)
            head_turn(8, 3)
            act.wait_ge(S("ofd_all"), 1)
            act.activation(hh[:, 0:H, NP_:T], ofd, ACT.Copy).then_inc(S("ofd_hi"), 1)

            with act.Fori(0, GH) as i:
                wait_apart(act, "hn_go", i + 1)
                act.activation(g_n[:, 0, :, :], z[:, ds(32 + 2 * i, 2), :], ACT.Square).then_inc(S("hn_sq"), 1)
                act.activation(g_n[:, 2, :, :], z[:, ds(40 + 2 * i, 2), :], ACT.Silu).then_inc(S("hn_silu"), 1)
                act.wait_ge(S("hn_ss"), i + 1)
                act.activation(rstd[:, :], bank[6][:, 0:T], ACT.Sqrt, bias=small[:, 7:8], scale=1.0 / DV).then_inc(S("hn_sqrt"), 1)
                wait_apart(act, "hn_out", i + 1)
                act.activation(hh[:, ds(8 + 2 * i, 2), :], g_n[:, 1, :, :], ACT.Copy).then_inc(S("hn_hi"), 1)

            cast(ST["out"][0], 0, 0, C)
            cast(ST["out"][0], 0, 1, C)
            casts("out")
            norm(2, T, 1, False)
            casts("xq")
            with act.Fori(0, XH) as i:
                f_stage(H + i, flat(x_q[:, ds(i, 1), 0:NP_]), flat(mkv[:, ds(XH + i, 1), :]))
                f_exp(H + i)
                f_pt(H + i)
                f_out_hi(H + i, i)
            for b in range(ND):
                act.wait_ge(S("xq_ps"), b + 1)
                if b >= 2:
                    act.wait_ge(S("xk_used"), b - 1)
                act.activation(x_qb[:, b % 2, :], bank[2 + b % 2][:, :], ACT.Copy, scale=SCALE).then_inc(S("xq_b"), 1)
            act.wait_ge(S("x_sub"), 1)
            act.activation(x_p[:, :, :, 0:XH], x_s, ACT.Exp).then_inc(S("x_exp"), 1)
            for b in range(ND):
                act.wait_ge(S("xv_used"), b + 1)
                if b >= 2:
                    act.wait_ge(S("xo_ps"), b - 1)
                act.activation(x_o[:, P * (b % 2):P * (b % 2) + P], bank[4 + 2 * (b % 2)][:, 0:P], ACT.Copy).then_inc(S("xo_sb"), 1)
            act.wait_ge(S("xod_ready"), 1)
            act.activation(hh[:, 0:XH, NP_:T], x_od, ACT.Copy).then_inc(S("xod_hi"), 1)
            casts("xo")
            norm(3, T, 3, False)

            def gate_up(half):
                name, (first, count, _) = f"gu{half}", ST[f"gu{half}"]

                def gu_step(i, k, blocks):
                    c = k // 2
                    chunk = HALF * half + 2 * i + c
                    if k % 2 == 0:
                        act.wait_ge(S("mm_done"), first + 4 * i + k + 1)
                        act.wait_ge(S("h_mul"), chunk + 1)
                        act.activation(f_sg[:, :], bank[0][:, 0:T], ACT.Silu).then_inc(S("acc0_free"), 1)
                        step(name, i, k, blocks)
                    else:
                        step(name, i, k, blocks)
                        wait_apart(act, "h_mul", chunk + 2)
                        act.activation(f_hi[:, ds(2 * i + c, 1), :], row(f_h[:, c, :]), ACT.Copy).then_inc(S("h_hi"), 1)
                for_panels(act, ch, name, gu_step)

            for half in range(2):
                gate_up(half)
                casts(f"dn{half}")
            norm(4, T, 4, False, final=True)
            act.wait_ge(S("out_act"), 48)
            act.wait_ge(S("stp_out"), 16 * GH + 16)

        @block.vector
        def _(dve):
            ch = Chain(dve, "dve_chain")
            tt, ts, stt = dve.tensor_tensor, dve.tensor_scalar, dve.scalar_tensor_tensor

            def split(first, i, k, blocks):
                dve.wait_ge(S("w_hi"), first + 4 * i + k + 1)
                tt(wlo[:, k % 4, 0:blocks * P], raw[:, k % 4, 0:blocks * P], whi[:, k % 2, 0:blocks * P], ALU.subtract
                   ).then_inc(S("w_split"), 1)

            def step(name, i, k, blocks, evac):
                first = ST[name][0]
                dve.wait_ge(S("mm_done"), first + 4 * i + k + 1)
                evac(i, k)
                if blocks:
                    split(first, i, k + 2, blocks)

            def panels(name, evac):
                for_panels(dve, ch, name, lambda i, k, b: step(name, i, k, b, evac))

            def to_z(tile0):
                return lambda i, k: dve.tensor_copy(z[:, ds(tile0 + 4 * i + k, 1), :], row(bank[k % 2][:, 0:T])
                                                    ).then_inc(S(f"acc{k % 2}_free"), 1)

            def add_x(i, k):
                xs = x_res[:, ds(4 * i + k, 1), :]
                tt(xs, row(bank[k % 2][:, 0:T]), xs, ALU.add).then_inc(S(f"acc{k % 2}_free"), 1)

            def own(sem, value):
                dve.wait_ge(S(sem), value)

            def norm(m, n, col, streamed, final=False):
                r = rstd[:, 0:n]
                if not streamed:
                    ch.link(dve.tensor_copy(sm8[:, 60:61], ones[:, 0:1]))
                    dve.sem_inc(S("n_go"), 1)
                dve.wait_ge(S("n_sqrt"), m + 1)
                ch.link(dve.reciprocal(r, r))
                rb = row(r).broadcast_to([P, 4, n])
                for g in range(4):
                    cur, xs = nb[:, g % 2, :, 0:n], x_res[:, 4 * g:4 * g + 4, :]
                    if final:
                        ch.link(tt(xs, xs, rb, ALU.mult))
                        tt(xs, xs, colv(gains[:, col, 4 * g:4 * g + 4]).broadcast_to([P, 4, n]), ALU.mult).then_inc(S("y_done"), 1)
                        continue
                    if streamed:
                        dve.wait_ge(S(f"nb_in{g % 2}"), 16 * (4 * m + 2 + g // 2 + 1))
                    elif g >= 2:
                        dve.wait_ge(S("n_hi"), 4 * m + g - 1)
                    tt(cur, cur if streamed else xs, rb, ALU.mult).then_inc(S("n_xn"), 1)
                    dve.wait_ge(S("n_hi"), 4 * m + g + 1)
                    for c in range(4):
                        ins = stt(hl[:, 4 * g + c, 0:n], nb[:, g % 2, c, 0:n], gains[:, col, 4 * g + c:4 * g + c + 1],
                                  hh[:, 4 * g + c, 0:n], ALU.mult, ALU.subtract)
                    ins.then_inc(S("n_lo_done"), 1)
                    own("n_lo_done", 4 * m + g + 1)

            for name in ("acc0_free", "acc1_free", "h_mul"):
                dve.sem_inc(S(name), 1)
            dve.memset(prob, 0.0)
            dve.wait_ge(S("nw_hi"), 1)
            tt(n_lo[:, :], n_raw[:, :], n_hi[:, :], ALU.subtract).then_inc(S("nw_lo"), 1)
            norm(0, T, 0, True)
            dve.wait_ge(S("nw_ps"), 1)
            ch.link(dve.tensor_copy(ggs[:, :], bank[7][0:RANK, 0:T]))
            u, ex = lf_t[:, 0, :], lf_t[:, 1, :]
            ch.link(ts(u, bank[7][32:32 + ND, 0:T], small[0:ND, 6:7], None, ALU.add))
            stt(ex, u, -1.0, u, ALU.mult, ALU.min).then_inc(S("lf_neg"), 1)
            dve.wait_ge(S("lf_ln"), 1)
            ch.link(stt(logf[:, :], u, 0.0, ex, ALU.min, ALU.subtract))
            ch.link(dve.tensor_tensor_scan(ndq[:, :], ones[0:ND, 0:1].broadcast_to([ND, NP_]), logf[:, 0:NP_], 0.0,
                                           ALU.mult, ALU.add))
            ch.link(ts(ndq[:, :], ndq[:, :], -1.0, None, ALU.mult))
            split(0, 0, 0, C)
            split(0, 0, 1, C)
            ch.link(tt(lf_in, colv(ident[0:ND, 0:H]).broadcast_to([ND, H, ND]), row(logf[:, NP_:T]).broadcast_to([ND, H, ND]), ALU.mult))
            dve.sem_inc(S("ds_in"), 1)

            def q_diag(t):
                tt(qd[:, :].rearrange("p (a b) -> p a b", a=H), row(ident).broadcast_to([P, H, P]),
                   z[:, 0:H, ds(NP_ + t, 1)].broadcast_to([P, H, P]), ALU.mult).then_inc(S("q_diag"), 1)

            tail4 = tail[:, :].rearrange("p (h b j) -> p j b h", h=H, b=ND)

            def k_page(t, j):
                q = j if isinstance(t, int) and t == 0 else MIX.index(("k", j))
                slot = q % SLOTS
                dve.wait_ge(S(f"page_in{slot}"), arrived(t, q))
                for h in range(H):
                    pk = page[:, slot, P * h:P * h + P]
                    ins = dve.tensor_tensor_reduce(out=pk, in0=pk, in1=qb[:, P * h:P * h + P], scale=1.0, scalar=0.0,
                                                   op0=ALU.mult, op1=ALU.add, accum_out=s_raw[:, j, h:h + 1])
                ins.then_inc(S("k_used"), 1)

            def s_max(t):
                own("k_used", 16 * t + 16)
                ch.link(tt(s_bias.rearrange("p (j b) h -> p j b h", b=1), s_raw.rearrange("p (j b) h -> p j b h", b=1),
                           tail4[:, :, ds(t, 1), :], ALU.add))
                ch.link(dve.tensor_reduce(sm8[:, 0:H], s_bias.rearrange("p j h -> p h j"), AX.X, ALU.max))
                tt(colv(sm8[:, 0:H]), colv(sm8[:, 0:H]), snew[:, :, ds(t, 1)], ALU.max).then_inc(S("mx_ready"), 1)

            def sm_diag(t):
                dve.wait_ge(S("mx_ps"), t)
                ch.link(dve.tensor_reduce(sm8[0:H, 40:41], bank[5][0:H, 0:P], AX.X, ALU.max))
                ts(sm8[0:H, 32:40], ident[0:H, 0:H], sm8[0:H, 40:41], None, ALU.mult).then_inc(S("m_diag"), 1)

            def sm_sub(t):
                dve.wait_ge(S("m_ps"), t)
                mb = bank[5][:, 128:136]
                ch.link(tt(s_bias, s_bias, row(mb).broadcast_to([P, PAGES, H]), ALU.subtract))
                tt(colv(sm8[:, 16:24]), snew[:, :, ds(t - 1, 1)], colv(mb), ALU.subtract).then_inc(S("s_sub"), 1)

            def sm_sum(t):
                dve.wait_ge(S("p_ready"), t)
                dve.tensor_reduce(sm8[:, 8:16], prob[:, :, 0:H].rearrange("p j h -> p h j"), AX.X, ALU.add
                                  ).then_inc(S("l_part"), 1)

            def sm_rec(t):
                dve.wait_ge(S("l_ps"), t)
                tt(sm8[:, 24:32], sm8[:, 16:24], bank[5][:, 136:144], ALU.add).then_inc(S("l_read"), 1)
                own("l_read", t)
                ch.link(dve.reciprocal(sm8[:, 24:32], sm8[:, 24:32]))

            def sm_out(t):
                dve.wait_ge(S("o_ps"), t)
                t8 = colv(sm8[:, 16:24])
                ch.link(tt(t8, t8, z[:, 2 * H:3 * H, ds(NP_ - 1 + t, 1)], ALU.mult))
                t42 = sm8[:, 16:24].rearrange("p (g e) -> p g e", e=2)
                ch.link(tt(t42, t42, bank[5][:, 144:152].rearrange("p (e g) -> p g e", e=2), ALU.add))
                ch.link(tt(ofd[:, :, ds(t - 1, 1)], t8, colv(sm8[:, 24:32]), ALU.mult))

            def fox_step(i, k, b):
                step("fox", i, k, b, to_z(0))

            some_panels(dve, 0, 2, fox_step)
            dve.wait_ge(S("gg_ps"), 1)
            for c in range(GH):
                ins = ts(g_t[:, 0, c, :], bank[2 + c][:, 0:T], small[:, 2 + c:3 + c], None, ALU.add)
            ch.link(ins)
            gu, ge = flat(g_t[:, 0, :, :]), flat(g_t[:, 1, :, :])
            stt(ge, gu, -1.0, gu, ALU.mult, ALU.min).then_inc(S("gg_neg"), 1)
            q_diag(0)
            dve.wait_ge(S("gg_ln"), 1)
            ch.link(stt(flat(g_t[:, 2, :, :]), gu, 0.0, ge, ALU.min, ALU.subtract))
            ts(flat(g_log), flat(g_t[:, 2, :, :]), 1.0 / 16.0, None, ALU.mult).then_inc(S("gates_done"), 1)
            for i in range(2, 6):
                for k in range(4):
                    fox_step(i, k, C)
                    if (i, k) == (2, 0):
                        dve.wait_ge(S("q_b"), 1)
                    if (i, k) == (3, 1):
                        dve.wait_ge(S("t_ps"), 1)
                        for n in range(2):
                            dve.tensor_copy(r_sb[:, 512 * n:512 * n + 512], bank[6 + n][:, :])
                        dve.tensor_copy(lfb, bank[5][:, 0:64].rearrange("p (a b) -> p a b", a=H)).then_inc(S("r_sb"), 1)
                        own("r_sb", 1)
                    if (i, k) == (4, 0):
                        ch.link(dve.tensor_copy(sm8[:, 60:61], ones[:, 0:1]))
                        tt(sq_in, z[:, 0:H, NP_:T], z[:, H:2 * H, NP_:T], ALU.mult).then_inc(S("sq_in"), 1)
                    if (i, k) == (4, 1):
                        dve.wait_ge(S("tail_ps"), 1)
                        for n in range(2):
                            ch.link(tt(tail[:, 512 * n:512 * n + 512].rearrange("p (a j) -> p a j", j=PAGES),
                                       bank[2 + n][:, :].rearrange("p (a j) -> p a j", j=PAGES),
                                       colv(flat(lfb)[:, 32 * n:32 * n + 32]).broadcast_to([P, 32, PAGES]), ALU.add))
                    if (i, k) == (5, 1):
                        dve.wait_ge(S("sq_ps"), 1)
                        ch.link(ts(snew, bank[5][:, 64:128].rearrange("p (a b) -> p a b", a=H), SCALE, None, ALU.mult))
                        dve.sem_inc(S("tail_ready"), 1)
                    k_page(0, 4 * i + k - 8)
            ch.link(dve.tensor_copy(sm8[:, 60:61], ones[:, 0:1]))
            dve.sem_inc(S("z_fox"), 1)
            s_max(0)
            q_diag(1)
            dve.wait_ge(S("g_eg"), 1)

            def panel_turn(t, evac, name, i0):
                def panel(k, blocks=C):
                    step(name, i0 + k // 4, k % 4, blocks, evac)
                last = name == "mem"
                dve.wait_ge(S("q_b"), t + 1)
                for k, piece in enumerate((sm_diag, sm_sub, sm_sum, sm_rec, None, None, None, None)):
                    k_page(t, 2 * k)
                    k_page(t, 2 * k + 1)
                    panel(k, 0 if last and k >= 6 else C)
                    if piece:
                        piece(t)
                    if k == 3:
                        q_diag(t + 1)
                sm_out(t)
                s_max(t)

            LINKS = 8
            first = ch.count
            with dve.Fori(1, 4) as t:
                ch.turn(first, t - 1, LINKS)
                panel_turn(t, to_z(24), "gla", 2 * t - 2)
            ch.after(first, 3, LINKS)
            norm(1, MEM, 2, True)
            panel_turn(4, lambda i, k: dve.tensor_copy(mkv[:, ds(4 * i + k, 1), :], row(bank[k % 2][:, 0:MEM])
                                                       ).then_inc(S(f"acc{k % 2}_free"), 1), "mem", 0)
            dve.sem_inc(S("mkv_done"), 1)
            ch.link(dve.memset(g_at, 0.0))
            for _ in range(2):
                dve.sem_inc(S("gs_free"), 1)

            def f_start(i, causal_):
                if causal_:
                    tt(row(a_nd[:, :]), row(ndq[:, :]), row(ident[0:ND, ds(i, 1)]).broadcast_to([ND, 1, NP_]), ALU.mult)
                    ch.link(dve.memset(a_s[:, 0, P:256], -1e30))
                dve.sem_inc(S("a_free"), 1)

            def f_max(n, causal_):
                dve.wait_ge(S("a_sc"), n + 1)
                if causal_:
                    tt(a_s[:, 0, 0:P], bank[6][:, 0:P], causal, ALU.add)
                    dve.tensor_copy(a_s[:, 1, 0:P], bank[6][:, 256:384])
                    ch.link(tt(a_s[:, 1, P:256], bank[6][:, 384:512], causal, ALU.add))
                else:
                    ch.link(dve.tensor_copy(flat(a_s), bank[6][:, :]))
                ch.link(dve.tensor_reduce(sm8[:, 48:50], a_s, AX.X, ALU.max))
                ts(sm8[:, 50:52], sm8[:, 48:50], -1.0, None, ALU.mult).then_inc(S("a_max"), 1)

            def f_scale(n):
                dve.wait_ge(S("a_exp"), n + 1)
                ch.link(dve.reciprocal(sm8[:, 54:56], sm8[:, 52:54]))
                for q in range(2):
                    ins = ts(a_s[:, q, :], a_s[:, q, :], sm8[:, 54 + q:55 + q], None, ALU.mult)
                ins.then_inc(S("a_p"), 1)

            def f_out(n):
                dve.wait_ge(S("a_ops"), n + 1)
                dve.tensor_copy(a_o[:, :], bank[7][:, 0:256]).then_inc(S("a_osb"), 1)

            def f_out_lo(n, i):
                dve.wait_ge(S("a_ohi"), n + 1)
                ch.link(tt(hl[:, ds(i, 1), 0:NP_], row(a_o[:, :]), hh[:, ds(i, 1), 0:NP_], ALU.subtract))

            def gd_start(b, s):
                dve.tensor_copy(colv(g_cols[:, s, 0, :]), z[:, 28:32, ds(NP_ + b, 1)])
                ts(colv(g_cols[:, s, 1, :]), z[:, 24:28, ds(NP_ + b, 1)], SCALE, None, ALU.mult)
                ch.link(dve.tensor_copy(colv(g_cols[:, s, 2, :]), g_eg[:, :, ds(b, 1)]))
                dve.sem_inc(S("gd_cols"), 1)
                tt(g_dd[:, :].rearrange("p (a b) -> p a b", a=8), row(ident).broadcast_to([P, 8, P]),
                   z[:, 32:40, ds(NP_ + b, 1)].broadcast_to([P, 8, P]), ALU.mult).then_inc(S("gd_diag"), 1)

            def gd_update(b, s):
                dve.wait_ge(S("gd_v"), b + 1)
                dve.wait_ge(S("gd_dec"), b + 1)
                for h in range(GH):
                    st = g_s[:, s, 256 * h:256 * h + 256]
                    ins = stt(st, bank[2 + h // 2][:, 256 * (h % 2):256 * (h % 2) + 256], g_cols[:, s, 0, h:h + 1], st, ALU.mult, ALU.add)
                ins.then_inc(S("gd_new"), 1)

            def gd_out(b):
                dve.wait_ge(S("gd_o"), b + 1)
                ch.link(dve.tensor_copy(g_ofd[:, :, ds(b, 1)], colv(bank[2][:, 0:8])))
                dve.sem_inc(S("gs_free"), 1)

            def halves(ap, l):
                half = 1 << l
                v = ap.rearrange("p (n two c) -> p n two c", two=2, c=half)
                return v[:, :, 0, :], v[:, :, 1, :]

            def g_diffs(i):
                dve.wait_ge(S("g_o"), i + 1)
                dve.sem_inc(S("g_free"), 1)
                ch.link(dve.tensor_tensor_scan(g_b, kst[:, K_SCAN:K_SCAN + NP_], flat(g_log[:, ds(i, 1), 0:NP_]), 0.0,
                                               ALU.mult, ALU.add))
                for l in range(LEVELS):
                    n, half = 256 >> (l + 1), 1 << l
                    lo, up = halves(g_b, l)
                    dlo, dup = halves(g_d[:, l, :], l)
                    ref = lo[:, :, half - 1:half].broadcast_to([P, n, half])
                    tt(dup, up, ref, ALU.subtract)
                    tt(dlo, ref, lo, ALU.subtract)
                b4 = g_b.rearrange("p (n c) -> p n c", c=64)
                tt(g_d[:, LEVELS, :].rearrange("p (n c) -> p n c", c=64), b4[:, :, 63:64].broadcast_to([P, 4, 64]), b4, ALU.subtract
                   ).then_inc(S("g_diff"), 1)

            def g_products(i):
                dve.wait_ge(S("g_exp"), i + 1)
                for l in range(LEVELS):
                    dlo, dup = halves(g_d[:, l, :], l)
                    klo, _ = halves(g_k, l)
                    _, qup = halves(g_q, l)
                    tt(dup, dup, qup, ALU.mult)
                    tt(dlo, dlo, klo, ALU.mult)
                tt(g_ke, g_d[:, LEVELS, :], g_k, ALU.mult)
                tt(g_qe, g_q, g_eb, ALU.mult).then_inc(S("g_qk"), 1)

            def g_levels(i, lo, hi):
                for l in range(lo, hi):
                    dve.wait_ge(S("g_aps"), (LEVELS + 1) * i + l + 1)
                    dve.tensor_copy(sm8[:, 60:61], ones[:, 0:1])
                    mask = masks[:, l * P:(l + 1) * P]
                    dve.copy_predicated(g_at, row(mask).broadcast_to([P, 2, P]), bank[l % 2][:, 0:256].rearrange("p (a b) -> p a b", a=2)
                                        ).then_inc(S("g_cp"), 1)
                    own("g_cp", (LEVELS + 1) * i + l + 1)

            def g_states(i):
                dve.wait_ge(S("g_kv"), i + 1)
                dve.wait_ge(S("stp_out"), 16 * i + 16)
                kv = [bank[c % 2][:, 256 * (c // 2):256 * (c // 2) + 256] for c in range(4)]
                ch.link(dve.tensor_copy(g_st[:, 0, :], kv[0]))
                for c in range(1, 4):
                    ch.link(stt(g_st[:, c, :], g_st[:, c - 1, :], g_eb[:, 64 * c + 63:64 * c + 64], kv[c], ALU.mult, ALU.add))
                dve.sem_inc(S("g_state"), 1)

            def head_turn(t, i):
                more = not (isinstance(t, int) and t == 8)

                def piece(j):
                    if j == 0:
                        sm_diag(t)
                        gd_start(2 * i, 0)
                    elif j == 1:
                        sm_sub(t)
                        f_start(2 * i, True)
                    elif j == 2:
                        g_diffs(i)
                    elif j == 3:
                        sm_sum(t)
                        gd_update(2 * i, 0)
                    elif j == 4:
                        sm_rec(t)
                        f_max(2 * i, True)
                    elif j == 5:
                        g_products(i)
                        gd_out(2 * i)
                        gd_start(2 * i + 1, 1)
                    elif j == 6:
                        f_scale(2 * i)
                    elif j == 7:
                        gd_update(2 * i + 1, 1)
                    elif j == 8:
                        g_levels(i, 0, 2)
                    elif j == 9:
                        f_out(2 * i)
                        gd_out(2 * i + 1)
                        if more and not (isinstance(t, int) and t == 7):
                            q_diag(t + 1)
                        g_levels(i, 2, 4)
                    elif j == 10:
                        f_out_lo(2 * i, 2 * i)
                        g_levels(i, 4, LEVELS + 1)
                    elif j == 11:
                        f_start(2 * i + 1, True)
                    elif j == 12:
                        g_states(i)
                    elif j == 13:
                        f_max(2 * i + 1, True)
                    elif j == 14:
                        f_scale(2 * i + 1)
                    else:
                        f_out(2 * i + 1)
                        sm_out(t)
                        if more:
                            s_max(t)
                        f_out_lo(2 * i + 1, 2 * i + 1)

                if more:
                    dve.wait_ge(S("q_b"), t + 1)
                for j in range(PAGES):
                    if more:
                        k_page(t, j)
                    piece(j)

            HLINKS = 27
            first = ch.count
            with dve.Fori(5, 7) as t:
                ch.turn(first, t - 5, HLINKS)
                head_turn(t, t - 5)
            ch.after(first, 2, HLINKS)
            head_turn(7, 2)
            head_turn(8, 3)
            dve.sem_inc(S("ofd_all"), 1)
            dve.wait_ge(S("ofd_hi"), 1)
            ch.link(tt(hl[:, 0:H, NP_:T], ofd, hh[:, 0:H, NP_:T], ALU.subtract))
            dve.wait_ge(S("g_o"), GH + 1)

            ch.link(dve.tensor_copy(z[:, 32:40, NP_:T], g_ofd))
            first = ch.count
            with dve.Fori(0, GH) as i:
                ch.turn(first, i, 3)
                dve.sem_inc(S("hn_go"), 1)
                dve.wait_ge(S("hn_sqrt"), i + 1)
                ch.link(dve.reciprocal(rstd[:, :], rstd[:, :]))
                dve.tensor_copy(g_n[:, 0, :, :], z[:, ds(32 + 2 * i, 2), :]).then_inc(S("hn_cp"), 1)
                own("hn_cp", i + 1)
                for j in range(2):
                    ins = stt(g_n[:, 1, j, :], g_n[:, 0, j, :], small[:, j:j + 1], rstd[:, :], ALU.mult, ALU.mult)
                ch.link(ins)
                dve.wait_ge(S("hn_silu"), i + 1)
                tt(g_n[:, 1, :, :], g_n[:, 1, :, :], g_n[:, 2, :, :], ALU.mult).then_inc(S("hn_out"), 1)
                dve.wait_ge(S("hn_hi"), i + 1)
                ch.link(tt(hl[:, ds(8 + 2 * i, 2), :], g_n[:, 1, :, :], hh[:, ds(8 + 2 * i, 2), :], ALU.subtract))
            ch.after(first, GH, 3)
            dve.wait_ge(S("out_act"), 48)
            dve.wait_ge(S("stp_out"), 16 * GH + 16)
            for s in range(2):
                dve.wait_ge(S(f"st_out{s}"), 16 * ND // 2 + 16)
            dve.sem_inc(S("gla_done"), 1)

            split(ST["out"][0], 0, 0, C)
            split(ST["out"][0], 0, 1, C)
            dve.wait_ge(S("x_in"), 16)
            panels("out", add_x)
            norm(2, T, 1, False)
            panels("xq", lambda i, k: dve.tensor_copy(x_q[:, k, :], bank[k % 2][:, 0:T]).then_inc(S(f"acc{k % 2}_free"), 1))
            ch.link(dve.memset(x_p, 0.0))
            first = ch.count
            with dve.Fori(0, XH) as i:
                ch.turn(first, i, 4)
                n = H + i
                f_start(i, False)
                f_max(n, False)
                f_scale(n)
                f_out(n)
                f_out_lo(n, i)
            ch.after(first, XH, 4)

            for b in range(ND):
                if b:
                    dve.wait_ge(S("xq_ps"), b)
                tt(x_qd[:, :].rearrange("p (a b) -> p a b", a=XH), row(ident).broadcast_to([P, XH, P]),
                   x_q[:, :, NP_ + b:NP_ + b + 1].broadcast_to([P, XH, P]), ALU.mult).then_inc(S("xq_diag"), 1)
                dve.wait_ge(S("xq_b"), b + 1)
                dve.wait_ge(S(f"page_in{b}"), 16 * 33)
                for m in range(2):
                    for h in range(XH):
                        pk = page[:, b, 512 * m + P * h:512 * m + P * h + P]
                        ins = dve.tensor_tensor_reduce(out=pk, in0=pk, in1=x_qb[:, b % 2, P * h:P * h + P], scale=1.0, scalar=0.0,
                                                       op0=ALU.mult, op1=ALU.add, accum_out=x_s[:, b, m, h:h + 1])
                ins.then_inc(S("xk_used"), 1)
            own("xk_used", ND)
            bh = "p (b h) -> p b h"
            tt(x_sm[:, 0:32].rearrange(bh, b=ND), x_s[:, :, 0, :], x_s[:, :, 1, :], ALU.max).then_inc(S("xmx_ready"), 1)
            dve.wait_ge(S("xmx_ps"), 1)
            ch.link(dve.tensor_reduce(x_sm[0:32, 64:65], bank[5][0:32, 0:P], AX.X, ALU.max))
            ts(x_sm[0:32, 96:128], ident[0:32, 0:32], x_sm[0:32, 64:65], None, ALU.mult).then_inc(S("xm_diag"), 1)
            dve.wait_ge(S("xm_ps"), 1)
            mb = bank[5][:, P:P + 32].rearrange(bh, b=ND)
            for m in range(2):
                ins = tt(x_s[:, :, m, :], x_s[:, :, m, :], mb, ALU.subtract)
            ins.then_inc(S("x_sub"), 1)
            dve.wait_ge(S("x_exp"), 1)
            tt(x_sm[:, 32:64].rearrange(bh, b=ND), x_p[:, :, 0, 0:XH], x_p[:, :, 1, 0:XH], ALU.add).then_inc(S("xl_part"), 1)
            dve.wait_ge(S("xl_ps"), 1)
            dve.reciprocal(x_sm[:, 128:160], bank[5][:, 160:192]).then_inc(S("xl_read"), 1)
            own("xl_read", 1)
            dve.wait_ge(S("xo_ps"), ND)
            tt(x_od.rearrange("p h b -> p b h"), bank[5][:, 192:224].rearrange(bh, b=ND), x_sm[:, 128:160].rearrange(bh, b=ND), ALU.mult
               ).then_inc(S("xod_ready"), 1)
            dve.wait_ge(S("xod_hi"), 1)
            ch.link(tt(hl[:, 0:XH, NP_:T], x_od, hh[:, 0:XH, NP_:T], ALU.subtract))
            dve.sem_inc(S("xo_go"), 1)
            panels("xo", add_x)
            norm(3, T, 3, False)

            def gate_up(half):
                name, (first, _, _) = f"gu{half}", ST[f"gu{half}"]

                def gu_step(i, k, blocks):
                    c = k // 2
                    chunk = HALF * half + 2 * i + c
                    dve.wait_ge(S("mm_done"), first + 4 * i + k + 1)
                    if k % 2 == 1:
                        dve.wait_ge(S("acc0_free"), (ACC[name] // 2) + 2 * i + c + 2)
                        tt(f_h[:, c, :], bank[1][:, 0:T], f_sg[:, :], ALU.mult).then_inc(S("h_mul"), 1)
                        own("h_mul", chunk + 2)
                        dve.sem_inc(S("acc1_free"), 1)
                    split(first, i, k + 2, blocks)
                    if k % 2 == 1:
                        dve.wait_ge(S("h_hi"), chunk + 1)
                        tt(f_lo[:, ds(2 * i + c, 1), :], row(f_h[:, c, :]), f_hi[:, ds(2 * i + c, 1), :], ALU.subtract).then_inc(S("h_lo"), 1)
                for_panels(dve, ch, name, gu_step)

            def add_down(i, k):
                if k % 2 == 1:
                    xs = x_res[:, ds(2 * i + k // 2, 1), :]
                    tt(xs, row(bank[k // 2][:, 0:T]), xs, ALU.add).then_inc(S(f"acc{k // 2}_free"), 1)

            for half in range(2):
                gate_up(half)
                panels(f"dn{half}", add_down)
            norm(4, T, 4, False, final=True)

        @block.tensor
        def _(pe):
            mm = pe.matmul

            def blk(t, slot, b):
                return t[:, slot, P * b:P * b + P]

            def three(out, k, b, rh, rl, start, stop):
                mm(out, blk(whi, k % 2, b), rh, start=start, stop=False)
                mm(out, blk(whi, k % 2, b), rl, start=False, stop=False)
                return mm(out, blk(wlo, k, b), rh, start=False, stop=stop)

            def panel(name, i, k, n=T):
                first, _, blocks = ST[name]
                pe.wait_ge(S("w_split"), first + 4 * i + k + 1)
                pe.wait_ge(S(f"acc{k % 2}_free"), ACC[name] // 2 + 2 * i + k // 2 + 1)
                for b in range(blocks):
                    last = three(bank[k % 2][:, 0:n], k, b, hh[:, b, 0:n], hl[:, b, 0:n], b == 0, b == blocks - 1)
                last.then_inc(S("mm_done"), 1)

            def panels(name, n=T):
                with pe.Fori(0, ST[name][1] // 4) as i:
                    for k in range(4):
                        panel(name, i, k, n)

            def norm(m, n):
                for g in range(4):
                    pe.wait_ge(S("n_sq"), 4 * m + g + 1)
                    for c in range(4):
                        last = mm(bank[6][:, 0:n], ones, nb[:, g % 2, c, 0:n], start=(g == 0 and c == 0), stop=(g == 3 and c == 3))
                    last.then_inc(S("n_ss"), 1)

            pe.wait_ge(S("params_in"), PARAMS)
            norm(0, T)
            pe.wait_ge(S("nw_lo"), 1)
            pe.wait_ge(S("n_lo_done"), 4)
            for b in range(C):
                w = slice(NARROW * b, NARROW * b + NARROW)
                mm(bank[7][0:NARROW, 0:T], n_hi[:, w], hh[:, b, :], start=b == 0, stop=False)
                mm(bank[7][0:NARROW, 0:T], n_hi[:, w], hl[:, b, :], start=False, stop=False)
                last = mm(bank[7][0:NARROW, 0:T], n_lo[:, w], hh[:, b, :], start=False, stop=b == C - 1)
            last.then_inc(S("nw_ps"), 1)

            def q_spread(t):
                pe.wait_ge(S("q_diag"), t + 1)
                for n in range(2):
                    last = mm(bank[2 + n][:, :], ones, qd[:, 512 * n:512 * n + 512], start=True, stop=True)
                last.then_inc(S("q_ps"), 1)

            def fox(i, k, b=None):
                panel("fox", i, k)

            some_panels(pe, 0, 2, fox)
            for c in range(GH):
                last = mm(bank[2 + c][:, 0:T], wgate[:, P * c:P * c + P], ggs[:, :], start=True, stop=True)
            last.then_inc(S("gg_ps"), 1)
            q_spread(0)
            for i in range(2, 6):
                for k in range(4):
                    fox(i, k)
                if i == 2:
                    pe.wait_ge(S("lf_in"), 16)
                    pe.wait_ge(S("ds_in"), 1)
                    pe.wait_ge(S("q_b"), 1)
                    fk = f_nat[:, :].rearrange("p (k h) -> p h k", h=H)
                    for h in range(H):
                        mm(bank[2 + h // 4][:, P * (h % 4):P * (h % 4) + P], fk[:, h, :], ident, start=True, stop=True)
                        mm(bank[6 + h // 4][:, P * (h % 4):P * (h % 4) + P], fk[:, h, :], later[:, P:2 * P], start=True, stop=True)
                    mm(bank[5][:, 0:64], ones[0:ND, :], flat(lf_in), start=True, stop=True).then_inc(S("t_ps"), 1)
                elif i == 3:
                    pe.wait_ge(S("t_sb"), 1)
                    pe.wait_ge(S("r_sb"), 1)
                    for n in range(2):
                        mm(bank[2 + n][:, :], later[:, 0:P], t_sb[:, 512 * n:512 * n + 512], start=True, stop=False)
                        last = mm(bank[2 + n][:, :], ones, r_sb[:, 512 * n:512 * n + 512], start=False, stop=True)
                    last.then_inc(S("tail_ps"), 1)
                elif i == 4:
                    pe.wait_ge(S("sq_in"), 1)
                    mm(bank[5][:, 64:128], ones, flat(sq_in), start=True, stop=True).then_inc(S("sq_ps"), 1)
            q_spread(1)

            def sm_mx(t):
                pe.wait_ge(S("mx_ready"), t)
                pe.transpose(bank[5][0:H, 0:P], sm8[:, 0:H], ident).then_inc(S("mx_ps"), 1)

            def sm_m(t):
                pe.wait_ge(S("m_diag"), t)
                mm(bank[5][:, 128:136], ones[0:H, :], sm8[0:H, 32:40], start=True, stop=True).then_inc(S("m_ps"), 1)

            def sm_l(t):
                pe.wait_ge(S("l_part"), t)
                mm(bank[5][:, 136:144], ones, sm8[:, 8:16], start=True, stop=True).then_inc(S("l_ps"), 1)

            def pv(t, lo, hi):
                for j in range(lo, hi):
                    q = MIX.index(("v", j)) if not (isinstance(t, int) and t == 8) else j
                    pe.wait_ge(S(f"page_in{q % SLOTS}"), arrived(t, q))
                    for g in range(4):
                        last = mm(bank[4][32 * g:32 * g + 32, 0:256], prob[:, j, :], page[:, q % SLOTS, 256 * g:256 * g + 256],
                                  start=j == 0, stop=j == PAGES - 1)
                    last.then_inc(S("v_used"), 1)

            def extract(t):
                pe.wait_ge(S("o_sb"), t)
                pe.wait_ge(S("l_read"), t)
                for e in range(2):
                    last = mm(bank[5][:, 144 + 4 * e:148 + 4 * e], osb[:, P * e:P * e + P], kst[:, K_SEL + 4 * e:K_SEL + 4 * e + 4],
                              start=True, stop=True)
                last.then_inc(S("o_ps"), 1)

            def panel_turn(t, name, i0, n):
                def one(k):
                    panel(name, i0 + k // 4, k % 4, n)
                one(0)
                sm_mx(t)
                one(1)
                sm_m(t)
                one(2)
                sm_l(t)
                one(3)
                pv(t, 0, 2)
                one(4)
                q_spread(t + 1)
                pv(t, 2, 6)
                one(5)
                pv(t, 6, 11)
                one(6)
                pv(t, 11, 16)
                one(7)
                extract(t)

            with pe.Fori(1, 4) as t:
                panel_turn(t, "gla", 2 * t - 2, T)
            norm(1, MEM)
            pe.wait_ge(S("n_lo_done"), 8)
            panel_turn(4, "mem", 0, MEM)

            def f_scores(n, kap, causal_):
                pe.wait_ge(S("a_staged"), n + 1)
                for q in range(2):
                    last = pe.transpose(bank[7][:, P * q:P * q + P], a_v[:, P * q:P * q + P], ident)
                last.then_inc(S("a_vps"), 1)
                if causal_:
                    for q in range(2):
                        w = P * (q + 1)
                        mm(bank[6][:, 256 * q:256 * q + w], a_q[:, P * q:P * q + P], kap(w), start=True, stop=False)
                        last = mm(bank[6][:, 256 * q:256 * q + w], ones[0:ND, :], a_nd[:, 0:w], start=False, stop=True)
                else:
                    for q in range(2):
                        last = mm(bank[6][:, 256 * q:256 * q + 256], a_q[:, P * q:P * q + P], kap(256), start=True, stop=True)
                last.then_inc(S("a_sc"), 1)

            def f_turned(n):
                pe.wait_ge(S("a_p"), n + 1)
                for kt in range(2):
                    for q in range(2):
                        last = pe.transpose(bank[6][:, 256 * kt + P * q:256 * kt + P * q + P], a_s[:, q, P * kt:P * kt + P], ident)
                last.then_inc(S("a_ptps"), 1)

            def f_out(n):
                pe.wait_ge(S("a_vn"), n + 1)
                pe.wait_ge(S("a_pt"), n + 1)
                mm(bank[7][:, 0:256], a_vn[:, 0, :], a_pt[:, 0, :], start=True, stop=False)
                mm(bank[7][:, 0:256], a_vn[:, 1, :], a_pt[:, 1, :], start=False, stop=True).then_inc(S("a_ops"), 1)

            def gd_spread(b):
                pe.wait_ge(S("gd_diag"), b + 1)
                for n in range(2):
                    last = mm(bank[2 + n][:, :], ones, g_dd[:, 512 * n:512 * n + 512], start=True, stop=True)
                last.then_inc(S("gd_v"), 1)

            def gd_query(b, s):
                pe.wait_ge(S("gd_new"), b + 1)
                for h in range(GH):
                    for j in range(2):
                        last = mm(bank[2][:, 2 * h + j:2 * h + j + 1], g_s[:, s, 256 * h + P * j:256 * h + P * j + P],
                                  g_cols[:, s, 1, h:h + 1], start=True, stop=True)
                last.then_inc(S("gd_o"), 1)

            def g_turn_v(i):
                pe.wait_ge(S("g_staged"), i + 1)
                for t in range(2):
                    for j in range(2):
                        last = pe.transpose(bank[0][:, 256 * t + P * j:256 * t + P * j + P], g_v[:, j, P * t:P * t + P], ident)
                last.then_inc(S("g_vps"), 1)

            def g_turn_k(i):
                pe.wait_ge(S("g_qk"), i + 1)
                for t in range(2):
                    last = pe.transpose(bank[1][:, P * t:P * t + P], g_ke[:, P * t:P * t + P], ident)
                last.then_inc(S("g_kps"), 1)

            def g_level(i, l):
                if l < 2:
                    pe.wait_ge(S(("g_vn", "g_kn")[l]), i + 1)
                else:
                    pe.wait_ge(S("g_cp"), (LEVELS + 1) * i + l - 1)
                k, q = (g_d[:, l, :], g_d[:, l, :]) if l < LEVELS else (g_k, g_q)
                for t in range(2):
                    last = mm(bank[l % 2][:, P * t:P * t + P], k[:, P * t:P * t + P], q[:, P * t:P * t + P], start=True, stop=True)
                last.then_inc(S("g_aps"), 1)

            def g_kv(i):
                pe.wait_ge(S("g_cp"), (LEVELS + 1) * (i + 1))
                for c in range(4):
                    r = slice(64 * (c % 2), 64 * (c % 2) + 64)
                    last = mm(bank[c % 2][:, 256 * (c // 2):256 * (c // 2) + 256], g_kn[r, c // 2, :], g_vn[r, c // 2, :],
                              start=True, stop=True)
                last.then_inc(S("g_kv"), 1)

            def g_out(i):
                pe.wait_ge(S("g_state"), i + 1)
                for j in range(2):
                    for t in range(2):
                        mm(bank[0][:, 256 * j + P * t:256 * j + P * t + P], g_vn[:, t, P * j:P * j + P], g_at[:, t, :],
                           start=t == 0, stop=False, skip_group_check=True)
                    for c in range(1, 4):
                        last = mm(bank[0][:, 256 * j + 64 * c:256 * j + 64 * c + 64], g_st[:, c - 1, P * j:P * j + P],
                                  g_qe[:, 64 * c:64 * c + 64], start=False, stop=c == 3, skip_group_check=True)
                last.then_inc(S("g_ops"), 1)

            def head_turn(t, i):
                def kap(c):
                    return lambda w: flat(z[:, ds(H + 2 * i + c, 1), 0:w])
                sm_mx(t)
                gd_spread(2 * i)
                sm_m(t)
                f_scores(2 * i, kap(0), True)
                g_turn_v(i)
                sm_l(t)
                gd_query(2 * i, 0)
                gd_spread(2 * i + 1)
                g_turn_k(i)
                g_level(i, 0)
                f_turned(2 * i)
                g_level(i, 1)
                gd_query(2 * i + 1, 1)
                f_out(2 * i)
                pv(t, 0, 2)
                g_level(i, 2)
                g_level(i, 3)
                pv(t, 2, 4)
                if not (isinstance(t, int) and t >= 7):
                    q_spread(t + 1)
                g_level(i, 4)
                g_level(i, 5)
                pv(t, 4, 6)
                g_level(i, 6)
                g_kv(i)
                pv(t, 6, 8)
                f_scores(2 * i + 1, kap(1), True)
                pv(t, 8, 10)
                g_out(i)
                pv(t, 10, 14)
                f_turned(2 * i + 1)
                pv(t, 14, 16)
                f_out(2 * i + 1)
                extract(t)

            with pe.Fori(5, 7) as t:
                head_turn(t, t - 5)
            head_turn(7, 2)
            head_turn(8, 3)
            with pe.Fori(0, GH) as i:
                pe.wait_ge(S("hn_sq"), i + 1)
                mm(bank[6][:, 0:T], ones, g_n[:, 0, 0, :], start=True, stop=False)
                mm(bank[6][:, 0:T], ones, g_n[:, 0, 1, :], start=False, stop=True).then_inc(S("hn_ss"), 1)

            pe.wait_ge(S("gla_done"), 1)
            panels("out")
            norm(2, T)
            pe.wait_ge(S("n_lo_done"), 12)
            panels("xq")
            with pe.Fori(0, XH) as i:
                f_scores(H + i, lambda w: flat(mkv[:, ds(i, 1), 0:w]), False)
                f_turned(H + i)
                f_out(H + i)
            for b in range(ND):
                pe.wait_ge(S("xq_diag"), b + 1)
                if b >= 2:
                    pe.wait_ge(S("xq_b"), b - 1)
                mm(bank[2 + b % 2][:, :], ones, x_qd[:, :], start=True, stop=True).then_inc(S("xq_ps"), 1)
            pe.wait_ge(S("xmx_ready"), 1)
            pe.transpose(bank[5][0:32, 0:P], x_sm[:, 0:32], ident).then_inc(S("xmx_ps"), 1)
            pe.wait_ge(S("xm_diag"), 1)
            mm(bank[5][:, P:P + 32], ones[0:32, :], x_sm[0:32, 96:128], start=True, stop=True).then_inc(S("xm_ps"), 1)
            pe.wait_ge(S("xl_part"), 1)
            mm(bank[5][:, 160:192], ones, x_sm[:, 32:64], start=True, stop=True).then_inc(S("xl_ps"), 1)
            for b in range(ND + 1):
                if b < ND:
                    pe.wait_ge(S(f"page_in{b}"), 16 * 34)
                    if b >= 2:
                        pe.wait_ge(S("xo_sb"), b - 1)
                    for m in range(2):
                        for g in range(4):
                            last = mm(bank[4 + 2 * (b % 2)][32 * g:32 * g + 32, 0:P], x_p[:, b, m, :],
                                      page[:, b, 512 * m + P * g:512 * m + P * g + P], start=m == 0, stop=m == 1)
                    last.then_inc(S("xv_used"), 1)
                if b:
                    pe.wait_ge(S("xo_sb"), b)
                    if b == 1:
                        pe.wait_ge(S("xl_read"), 1)
                    c = b - 1
                    mm(bank[5][:, 192 + 4 * c:196 + 4 * c], x_o[:, P * (c % 2):P * (c % 2) + P], kst[:, K_SEL + 8:K_SEL + 12],
                       start=True, stop=True).then_inc(S("xo_ps"), 1)
            pe.wait_ge(S("xo_go"), 1)
            panels("xo")
            norm(3, T)
            pe.wait_ge(S("n_lo_done"), 16)
            for half in range(2):
                panels(f"gu{half}")
                name = f"dn{half}"
                first = ST[name][0]
                pe.wait_ge(S("h_lo"), HALF * (half + 1))
                with pe.Fori(0, 8) as i:
                    for k in range(4):
                        pe.wait_ge(S("w_split"), first + 4 * i + k + 1)
                        if k % 2 == 0:
                            pe.wait_ge(S(f"acc{k // 2}_free"), ACC[name] // 2 + i + 1)
                        for b in range(SUB):
                            kk = SUB * (k % 2) + b
                            last = three(bank[k // 2][:, 0:T], k, b, f_hi[:, kk, :], f_lo[:, kk, :], kk == 0, kk == HALF - 1)
                        last.then_inc(S("mm_done"), 1)
            norm(4, T)


def panels_of(w):
    k, n = w.shape
    return np.ascontiguousarray(w.reshape(k // P, P, n // P, P).transpose(2, 1, 0, 3).reshape(n, k))


def chunks_of(a):
    return np.ascontiguousarray(a.T.reshape(-1, P, a.shape[0]).transpose(1, 0, 2).reshape(P, -1))


def kernel(**x):
    import concourse.bacc as bacc
    from concourse.bass_utils import run_bass_kernel_spmd

    x = {n: np.asarray(a) for n, a in x.items()}
    w_in = x["w_in"][0]
    splits = np.cumsum((1024, 1024, 1024, 8, 512, 512, 1024, 1024, 16))
    narrow = np.zeros((D, NARROW), np.float32)
    narrow[:, 0:RANK] = w_in[:, splits[7]:splits[8]]
    narrow[:, 32:40] = w_in[:, splits[2]:splits[3]]
    gate, up = panels_of(x["w_ffn_gate"][0]), panels_of(x["w_ffn_up"][0])
    gu = np.stack([gate.reshape(-1, P, D), up.reshape(-1, P, D)], 1).reshape(-1, D)
    down = x["w_ffn_down"][0].reshape(2, 2, SUB, P, C, P).transpose(0, 4, 1, 3, 2, 5).reshape(-1, SUB * P)
    kst, later, masks = constants()
    small = np.zeros((P, 8), np.float32)
    small[:, 0:2] = x["g_gla_head"][0].reshape(2, P).T
    small[:, 2:6] = x["b_gla_gate"][0].reshape(4, P).T
    small[0:H, 6] = x["b_forget"][0]
    small[:, 7] = EPS
    n_pool = x["cache_fox_k"].shape[1]
    ins = {
        "x_fm": chunks_of(np.concatenate([x["x_prompt"][0], x["x_sample"][:, 0]])),
        "mem_fm": chunks_of(x["mem_prompt"][0]),
        "gains": np.concatenate([g.reshape(C, P).T for g in (x["g_mix"], x["g_cross"], x["g_mem"], x["g_ffn"], x["g_final"])], 1),
        "kst": kst, "masks": masks, "later": later, "small": small, "wgate": x["w_gla_gate"][0],
        "w_narrow": narrow.reshape(C, P, NARROW).transpose(1, 0, 2).reshape(P, -1),
        "p_fox": panels_of(w_in[:, 0:splits[2]]), "p_gla": panels_of(w_in[:, splits[3]:splits[7]]),
        "p_mem": np.concatenate([panels_of(x["w_xk"][0]), panels_of(x["w_xv"][0])]),
        "p_out": panels_of(x["w_out"][0]), "p_xq": panels_of(x["w_xq"][0]), "p_xo": panels_of(x["w_xo"][0]),
        "p_gu0": gu[0:len(gu) // 2], "p_gu1": gu[len(gu) // 2:], "p_dn0": down[0:len(down) // 2], "p_dn1": down[len(down) // 2:],
        "kc": x["cache_fox_k"].reshape(n_pool * PAGE, H * P), "vc": x["cache_fox_v"].reshape(n_pool * PAGE, H * P),
        "lf": x["cache_fox_logf"].reshape(n_pool, PAGE * H),
        "pt_row": x["page_table"].reshape(1, -1), "pt_col": x["page_table"].reshape(-1, 1),
        "s0": x["state_gla"].reshape(-1, DV), "cmk": x["cache_mem_k"].reshape(-1, XH * P), "cmv": x["cache_mem_v"].reshape(-1, XH * P),
    }
    outs = {"o_y": (P, C * T), "o_kv": (P, 2 * H * T), "o_logf": (ND, T), "o_stp": (GH * P, DV), "o_mkv": (P, 2 * XH * MEM),
            "o_sts": (ND * GH * P, DV)}
    nc = bacc.Bacc("TRN2", target_bir_lowering=False, num_devices=1)
    arrays, io = {}, {"n_pool": n_pool}
    for name, a in ins.items():
        arrays[name + "_dram"] = np.ascontiguousarray(a)
        io[name] = nc.dram_tensor(name + "_dram", a.shape, mybir.dt.from_np(a.dtype), kind="ExternalInput").ap()
    for name, shape in outs.items():
        io[name] = nc.dram_tensor(name + "_dram", shape, mybir.dt.float32, kind="ExternalOutput").ap()
    build(nc, io)
    r = run_bass_kernel_spmd(nc, [arrays], core_ids=[0]).results[0]
    r = {name: np.asarray(r[name + "_dram"]) for name in outs}

    y = r["o_y"].reshape(P, C, T).transpose(2, 1, 0).reshape(T, D)
    kv = r["o_kv"].reshape(P, 2, H, T).transpose(1, 3, 2, 0)
    lf = r["o_logf"].T
    mkv = r["o_mkv"].reshape(P, 2, XH, MEM).transpose(1, 3, 2, 0)
    c = np.ascontiguousarray
    return (c(y[0:NP_])[None], c(y[NP_:])[:, None],
            c(kv[0, 0:NP_])[None, None], c(kv[1, 0:NP_])[None, None], c(lf[0:NP_])[None, None],
            r["o_stp"].reshape(1, 1, GH, P, DV), c(mkv[0])[None, None], c(mkv[1])[None, None],
            c(kv[0, NP_:])[None, :, None], c(kv[1, NP_:])[None, :, None], c(lf[NP_:])[None, :, None],
            r["o_sts"].reshape(1, ND, GH, P, DV))
```

```python
from contextlib import ExitStack

import numpy as np
import concourse.bass as bass
from concourse import mybir
from concourse.alu_op_type import AluOpType as ALU

P = 128
D = 2048
NP_ = 256
ND = 8
T = NP_ + ND
C = D // P
H = 8
PAGES = 16
PAGE = 128
GH = 4
DV = 256
XH = 4
MEM = 256
FFN = 5632
HALF = FFN // P // 2
SUB = HALF // 2
RANK = 16
LEVELS = 6
EPS = 1e-6
SCALE = float(P) ** -0.5
NARROW = 40

SLOTS = 8
MIX = [("k", j) for j in range(8)] + [x for j in range(8) for x in (("v", 2 * j), ("v", 2 * j + 1), ("k", 8 + j))]

K_ID, K_ONE, K_CAUS, K_SEL, K_SCAN = 0, P, 2 * P, 3 * P, 3 * P + 16
K_ALL = K_SCAN + NP_


def constants():
    k = np.zeros((P, K_ALL), np.float32)
    r = np.arange(P)
    k[:, K_ID:K_ID + P] = np.eye(P)
    k[:, K_ONE:K_ONE + P] = 1.0
    k[:, K_CAUS:K_CAUS + P] = np.where(r[None, :] <= r[:, None], 0.0, -1e30)
    for g in range(4):
        k[32 * g + 2 * g, K_SEL + g] = 1.0
        k[32 * g + 2 * g + 1, K_SEL + 4 + g] = 1.0
        k[32 * g + g, K_SEL + 8 + g] = 1.0
    k[:, K_SCAN:K_SCAN + NP_] = (np.arange(NP_) % 64 != 0)[None, :]
    s, t = r[:, None], r[None, :]
    masks = np.zeros((P, LEVELS + 1, P), np.uint8)
    for l in range(LEVELS):
        b = 2 << l
        masks[:, l] = (s // b == t // b) & (s % b < b // 2) & (t % b >= b // 2)
    masks[:, LEVELS] = s == t
    later = np.zeros((P, 2, P), np.float32)
    later[:, 0] = s > t
    later[:, 1] = (s // PAGES == t // PAGES) & (s % PAGES > t % PAGES)
    return k, later.reshape(P, 2 * P), masks.reshape(P, -1).view(np.int32)


ST = {}


def _stages():
    n = 0
    for name, count, blocks in (("fox", 24, C), ("gla", 24, C), ("mem", 8, C), ("out", 16, C), ("xq", 4, C), ("xo", 4, C),
                                ("gu0", 2 * HALF, C), ("dn0", 32, SUB), ("gu1", 2 * HALF, C), ("dn1", 32, SUB)):
        ST[name] = (n, count, blocks)
        n += count
    return n


N_PANELS = _stages()
ORDER = list(ST)


def acc_count():
    out, a = {}, 0
    for name in ORDER:
        out[name] = a
        a += C if name == "xo" else ST[name][1] // (2 if name.startswith("dn") else 1)
    return out


ACC = acc_count()


def build(nc, io):
    f32, f32r, i32 = mybir.dt.float32, mybir.dt.float32r, mybir.dt.int32
    ACT = mybir.ActivationFunctionType
    AX = mybir.AxisListType
    ds = bass.ds

    base = (nc.sbuf_base + 63) // 64 * 64

    def at(name, off, shape, dt=f32):
        return nc.alloc_sbuf_tensor_at(name, [shape[0], int(np.prod(shape[1:]))], dt, offset=base + off)

    def view(t, *dims):
        names = "abcd"[:len(dims)]
        if len(dims) == 1:
            return t[:, :]
        return t[:, :].rearrange(f"p ({' '.join(names)}) -> p {' '.join(names)}", **{n: d for n, d in zip(names, dims)})

    A0 = 0
    B0 = A0 + C * T * 4
    C0 = B0 + 2 * C * T * 4
    D0 = C0 + 48 * T * 4
    E0 = D0 + 6 * C * P * 4
    F0 = E0 + SLOTS * 1024 * 4
    G0 = F0 + 2 * XH * MEM * 4
    H0 = G0 + 2 * 4 * T * 4 + T * 4
    TW = T * 4

    x_res = view(at("x_res", A0, [P, C, T]), C, T)
    hh = view(at("hh", B0, [P, C, T], f32r), C, T)
    hl = view(at("hl", B0 + C * TW, [P, C, T], f32r), C, T)
    z = view(at("z", C0, [P, 48, T]), 48, T)
    raw = view(at("raw", D0, [P, 4, C * P]), 4, C * P)
    whi = view(at("whi", D0 + 4 * C * P * 4, [P, 2, C * P], f32r), 2, C * P)
    wlo = view(at("wlo", D0, [P, 4, C * P], f32r), 4, C * P)
    page = view(at("page", E0, [P, SLOTS, 1024]), SLOTS, 1024)
    mkv = view(at("mkv", F0, [P, 2 * XH, MEM]), 2 * XH, MEM)
    nb = view(at("nb", G0, [P, 2, 4, T]), 2, 4, T)
    rstd = at("rstd", G0 + 8 * TW, [P, T])
    o = H0

    def keep(name, *dims, parts=P, dt=f32):
        nonlocal o
        t = at(name, o, [parts, *dims], dt)
        o += (int(np.prod(dims)) * 4 + 31) // 32 * 32
        return t
    kst = keep("kst", K_ALL)
    masks4 = keep("masks", (LEVELS + 1) * P // 4, dt=i32)
    masks = masks4[:, :].bitcast(mybir.dt.uint8)
    gains = view(keep("gains", 5, C), 5, C)
    small = keep("small", 8)
    g_log = view(keep("g_log", GH, T), GH, T)
    logf = keep("logf", T, parts=ND)
    ndq = keep("ndq", NP_, parts=ND)
    pts = keep("pts", P, parts=1, dt=i32)
    ptc = keep("ptc", 1, dt=i32)
    snew = view(keep("snew", H, ND), H, ND)
    ofd = view(keep("ofd", H, ND), H, ND)
    sm8 = keep("sm8", 64)
    assert base + o <= nc.sbuf_usable_end, (base + o, nc.sbuf_usable_end)
    ident, ones = kst[:, K_ID:K_ID + P], kst[:, K_ONE:K_ONE + P]
    causal = kst[:, K_CAUS:K_CAUS + P]

    qd = at("qd", A0, [P, 1024])
    qb = at("qb", A0 + 4096, [P, 1024])
    tail = at("tail", A0 + 8192, [P, 1024])
    prob = view(at("prob", A0 + 12288, [P, PAGES, 32]), PAGES, 32)
    s_raw = view(at("s_raw", A0 + 14336, [P, PAGES, H]), PAGES, H)
    s_bias = view(at("s_bias", A0 + 14848, [P, PAGES, H]), PAGES, H)
    osb = at("osb", A0 + 15360, [P, 256])
    g_ofd = view(at("g_ofd", A0 + 16384, [P, 8, ND]), 8, ND)
    g_eg = view(at("g_eg", A0 + 16640, [P, GH, ND]), GH, ND)
    f_nat = at("f_nat", F0, [P, 1024])
    t_sb = at("t_sb", F0 + 4096, [P, 1024])
    r_sb = at("r_sb", G0, [P, 1024])
    lf_in = view(at("lf_in", G0 + 4096, [ND, H, ND]), H, ND)
    sq_in = view(at("sq_in", G0 + 4608, [P, H, ND]), H, ND)
    lfb = view(at("lfb", G0 + 7232, [P, H, ND]), H, ND)
    lf_t = view(at("lf_t", G0 + 5120, [ND, 2, T]), 2, T)
    later = at("later", C0 + 47 * TW, [P, 256])
    wgate = at("wgate", C0 + 36 * TW, [RANK, 4 * P])
    ggs = at("ggs", G0, [RANK, T])
    n_raw = at("n_raw", C0 + 41 * TW, [P, C * NARROW])
    n_hi = at("n_hi", C0 + 44 * TW, [P, C * NARROW], f32r)
    n_lo = at("n_lo", C0 + 38 * TW, [P, C * NARROW], f32r)
    assert C * NARROW * 4 <= 3 * TW
    def attention_set(x, off, cols):
        return (at("a_q" + x, off, [P, 256]), at("a_v" + x, off + 1024, [P, 256]),
                view(at("a_vn" + x, off + 2048, [P, 2, P]), 2, P), view(at("a_s" + x, off + 3072, [P, 2, 256]), 2, 256),
                view(at("a_pt" + x, off + 5120, [P, 2, 256]), 2, 256), cols)
    A_SETS = (attention_set("0", G0, 48), attention_set("1", C0 + 16 * TW, 40))
    a_nd = at("a_nd", G0 + 8192, [ND, 256])
    s_acc, s_sq = at("s_acc", G0 + 4 * TW, [P, T]), at("s_sq", G0 + 5 * TW, [P, T])
    o_d = 0

    def in_ring(name, *dims):
        nonlocal o_d
        t = at(name, D0 + o_d, [P, *dims])
        o_d += (int(np.prod(dims)) * 4 + 31) // 32 * 32
        assert o_d <= 6 * C * P * 4
        return view(t, *dims)
    g_v, g_vn, g_kn, g_at = in_ring("g_v", 2, 256), in_ring("g_vn", 2, 256), in_ring("g_kn", 2, P), in_ring("g_at", 2, P)
    g_st = in_ring("g_st", 4, 256)
    g_b, g_kq = in_ring("g_b", 256), in_ring("g_kq", 512)
    g_k, g_q = g_kq[:, 0:256], g_kq[:, 256:512]
    g_eb, g_ke, g_qe = in_ring("g_eb", 256), in_ring("g_ke", 256), in_ring("g_qe", 256)
    g_d = in_ring("g_d", LEVELS + 1, 256)
    g_dd = in_ring("g_dd", 1024)
    g_s = in_ring("g_s", 2, 1024)
    g_cols = in_ring("g_cols", 2, 3, GH)
    g_t = view(at("g_t", C0 + 24 * TW, [P, 3, GH, T]), 3, GH, T)
    g_sq = view(at("g_sq", C0, [P, 2 * GH, T]), 2 * GH, T)
    g_rs = view(at("g_rs", C0 + 24 * TW, [P, GH, T]), GH, T)
    f_hi = view(at("f_hi", C0, [P, HALF, T], f32r), HALF, T)
    f_lo = view(at("f_lo", C0 + HALF * TW, [P, HALF, T], f32r), HALF, T)
    f_sg = at("f_sg", G0, [P, T])
    f_h = view(at("f_h", G0 + TW, [P, 2, T]), 2, T)
    x_q = view(at("x_q", C0, [P, XH, T]), XH, T)
    x_qd = at("x_qd", C0 + 4 * TW, [P, 512])
    x_qb = view(at("x_qb", C0 + 6 * TW, [P, 2, 512]), 2, 512)
    x_s = view(at("x_s", C0 + 10 * TW, [P, ND, 2, XH]), ND, 2, XH)
    x_p = view(at("x_p", C0 + 11 * TW, [P, ND, 2, 32]), ND, 2, 32)
    x_o = at("x_o", C0 + 13 * TW, [P, 256])
    x_sm = at("x_sm", C0 + 14 * TW, [P, 256])
    x_od = view(at("x_od", C0 + 15 * TW, [P, XH, ND]), XH, ND)

    ctx = ExitStack()
    with ctx:
        bank = [ctx.enter_context(nc.psum_tensor(f"bank{i}", [P, 512], f32)) for i in range(8)]
        sems = {}
        PARAMS = 16 * 7

        def S(name):
            if name not in sems:
                sems[name] = ctx.enter_context(nc.semaphore(name))
            return sems[name]

        block = ctx.enter_context(nc.Block())

        def wait_apart(eng, sem, value):
            eng.wait_ge(S("params_in"), PARAMS)
            eng.wait_ge(S(sem), value)

        class Chain:
            def __init__(self, eng, name):
                self.eng, self.sem, self.start, self.n = eng, S(name), 0, 0

            def link(self, ins):
                self.n += 1
                ins.then_inc(self.sem, 1)
                self.eng.wait_ge(self.sem, self.start + self.n)

            def turn(self, first, i, per_turn):
                self.start, self.n = first + i * per_turn, 0

            def after(self, first, turns, per_turn):
                assert self.n == per_turn, (self.n, per_turn)
                self.start, self.n = first + turns * per_turn, 0

            @property
            def count(self):
                return self.start + self.n


        def row(ap):
            return ap.rearrange("p (a b) -> p a b", a=1)

        def flat(ap):
            return ap.rearrange("p a b -> p (a b)")

        @block.sync
        def _(sp):
            x_fm = io["x_fm"].rearrange("p (a b) -> p a b", a=C)

            def first_x(g):
                sp.dma_start(x_res[:, 4 * g:4 * g + 4, :], x_fm[:, 4 * g:4 * g + 4, :]).then_inc(S(f"first_x{g}"), 16)

            first_x(0)
            for dst, src in ((kst[:, :], "kst"), (small[:, :], "small"), (gains.rearrange("p a b -> p (a b)"), "gains"), (n_raw[:, :], "w_narrow"),
                             (masks4[:, :], "masks"), (wgate[:, :], "wgate"), (later[:, :], "later")):
                sp.dma_start(dst, io[src]).then_inc(S("params_in"), 16)
            for g in range(1, 4):
                first_x(g)
            mem_fm = io["mem_fm"].rearrange("p (a b) -> p a b", a=C)

            def stream(lo, hi):
                for g in range(lo, hi):
                    if 2 <= g < 6:
                        sp.wait_ge(S("n_ss"), 4 + min(g - 1, 4))
                    elif g >= 6:
                        sp.wait_ge(S("n_lo_done"), 4 + g - 5)
                    sp.dma_start(nb[:, g % 2, :, 0:MEM], mem_fm[:, 4 * (g % 4):4 * (g % 4) + 4, :]).then_inc(S(f"nb_in{g % 2}"), 16)

            def load(name, i, k):
                first, count, blocks = ST[name]
                if not (first == 0 and isinstance(i, int) and i == 0):
                    sp.wait_ge(S("mm_done"), first + 4 * i + k - 3)
                sp.dma_start(raw[:, k, 0:blocks * P], io["p_" + name][ds((4 * i + k) * P, P), :]).then_inc(S(f"w_in{k}"), 16)

            def loads(name, lo=0):
                with sp.Fori(lo, ST[name][1] // 4) as i:
                    for k in range(4):
                        load(name, i, k)

            for k in range(4):
                load("fox", 0, k)
            loads("fox", 1)
            for k in range(4):
                load("gla", 0, k)
            sp.wait_ge(S("tail_ready"), 1)
            stream(0, 2)
            for k in range(4):
                load("gla", 1, k)
            stream(2, 4)
            for k in range(4):
                load("gla", 2, k)
            stream(4, 6)
            loads("gla", 3)
            for k in range(4):
                load("mem", 0, k)
            stream(6, 8)
            for k in range(4):
                load("mem", 1, k)
            sp.wait_ge(S("ring_free"), 1)
            for k in range(4):
                load("out", 0, k)
            sp.wait_ge(S("hn_go"), 1)
            sp.dma_start(x_res, x_fm).then_inc(S("x_in"), 16)
            loads("out", 1)
            for k in range(4):
                load("xq", 0, k)
            for name in ORDER[5:]:
                loads(name)
            for g in range(4):
                sp.wait_ge(S("y_done"), g + 1)
                sp.dma_start(io["o_y"][:, 4 * g * T:4 * (g + 1) * T], flat(x_res[:, 4 * g:4 * g + 4, :])).then_inc(S("y_out"), 16)
            sp.wait_ge(S("y_out"), 64)

        @block.gpsimd
        def _(pool):
            pool.dma_start(pts[:, :], io["pt_row"]).then_inc(S("pt_in"), 16)
            pool.dma_start(ptc[:, :], io["pt_col"]).then_inc(S("pt_in"), 16)
            pool.wait_ge(S("pt_in"), 32)
            pool.indirect_dma_start(f_nat[:, :], None, io["lf"], bass.IndirectOffsetOnAxis(ap=ptc[:, 0:1], axis=0)
                                    ).then_inc(S("lf_in"), 16)

            def fetch(src, index, slot, sem=None, value=0):
                r = pool.value_load(pts[0:1, ds(index, 1)], min_val=0, max_val=io["n_pool"] - 1)
                if sem:
                    pool.wait_ge(S(sem), value)
                pool.dma_start(page[:, slot, :], io[src][ds(r * P, P), :]).then_inc(S(f"page_in{slot}"), 16)

            pool.wait_ge(S("n_sq"), 4)
            for j in range(8):
                fetch("kc", j, j)
            for j in range(8, 16):
                fetch("kc", j, j - 8, "k_used", j - 7)

            def mixed(t, q):
                if q >= SLOTS:
                    kind, j, turn = *MIX[q - SLOTS], t
                elif isinstance(t, int):
                    kind, j, turn = "k", 16 - SLOTS + q, 0
                else:
                    kind, j, turn = *MIX[q + 32 - SLOTS], t - 1
                sem, value = ("k_used", 16 * turn + j + 1) if kind == "k" else ("v_used", 16 * turn - 15 + j)
                now, j = MIX[q]
                fetch("kc" if now == "k" else "vc", 16 * t + j if now == "k" else 16 * t - 16 + j, q % SLOTS, sem, value)

            for q in range(32):
                mixed(1, q)
            with pool.Fori(2, 8) as t:
                for q in range(32):
                    mixed(t, q)
            for j in range(16):
                if j < SLOTS:
                    kind, i = MIX[32 - SLOTS + j]
                    fetch("vc", 112 + j, j, *(("k_used", 113 + i) if kind == "k" else ("v_used", 97 + i)))
                else:
                    fetch("vc", 112 + j, j - SLOTS, "v_used", 113 + j - SLOTS)
            ck = io["cmk"].rearrange("(b m p) n -> b p m n", p=P, m=2)
            cv = io["cmv"].rearrange("(b m p) n -> b p m n", p=P, m=2)
            def cross_page(b):
                if b < 8:
                    pool.wait_ge(S("v_used"), 121 + b)
                else:
                    pool.wait_ge(S("xk_used"), b - 7)
                pool.dma_start(page[:, b % 8, :].rearrange("p (m n) -> p m n", m=2), (ck if b < 8 else cv)[b % 8]
                               ).then_inc(S(f"page_in{b % 8}"), 16)

            def square_sums(m, name, go, value):
                pch = Chain(pool, f"pool_chain{m}")
                pool.wait_ge(S(go), value)
                pch.link(pool.memset(s_acc[:, :], 0.0))
                per = 2 if name.startswith("dn") else 4
                start = pch.count
                with pool.Fori(0, C // per) as i:
                    pch.turn(start, i, 2 * per)
                    for j in range(per):
                        pool.wait_ge(S(f"acc{j % 2}_free"), ACC[name] // 2 + (per // 2) * i + j // 2 + 2)
                        xs = x_res[:, ds(per * i + j, 1), :]
                        pch.link(pool.tensor_tensor(row(s_sq[:, :]), xs, xs, ALU.mult))
                        pch.link(pool.tensor_tensor(s_acc[:, :], s_acc[:, :], s_sq[:, :], ALU.add))
                pool.sem_inc(S("n_acc"), 1)

            for b in range(8):
                cross_page(b)
            square_sums(2, "out", "gla_done", 1)
            for b in range(8, 16):
                cross_page(b)
            square_sums(3, "xo", "xo_go", 1)
            square_sums(4, "dn1", "n_lo_done", 16)

        def arrived(t, q):
            return 16 * (q // 8 + 1) if isinstance(t, int) and t == 0 else 64 * t - 32 + 16 * (q // 8 + 1)

        HN_BANKS = (2, 3, 6, 7)

        def a_set(n):
            c = 0 if not isinstance(n, int) or n < H else n % 2
            return (*A_SETS[c], bank[(6, 0)[c]], bank[(7, 1)[c]])

        def x_bank(b):
            return bank[4 - b % 2]


        def colv(ap):
            return ap.rearrange("p (a b) -> p a b", b=1)

        def blocks_after(name):
            p = ORDER.index(name) + 1
            return ST[ORDER[p]][2] if p < len(ORDER) else 0

        def some_panels(eng, lo, hi, step):
            with eng.Fori(lo, hi) as i:
                for k in range(4):
                    step(i, k, C)

        def for_panels(eng, ch, name, step, links=0):
            first, count, blocks = ST[name]
            nxt, links0 = blocks_after(name), ch.count
            if count > 4:
                with eng.Fori(0, count // 4 - 1) as i:
                    ch.turn(links0, i, links)
                    for k in range(4):
                        step(i, k, blocks)
                ch.after(links0, count // 4 - 1, links)
            for k in range(4):
                step(count // 4 - 1, k, blocks if k < 2 else nxt)

        @block.scalar
        def _(act):
            ch = Chain(act, "act_chain")

            def cast(first, i, k, blocks):
                kk, ii = k % 4, i + k // 4
                act.wait_ge(S(f"w_in{kk}"), 16 * (ii + first // 4 + 1))
                act.activation(whi[:, kk % 2, 0:blocks * P], raw[:, kk, 0:blocks * P], ACT.Copy).then_inc(S("w_hi"), 1)

            def step(name, i, k, blocks):
                first = ST[name][0]
                act.wait_ge(S("mm_done"), first + 4 * i + k + 1)
                if blocks:
                    cast(first, i, k + 2, blocks)

            def casts(name):
                for_panels(act, ch, name, lambda i, k, b: step(name, i, k, b))

            def norm_root(m, n):
                act.wait_ge(S("n_ss"), 4 * m + 4)
                act.activation(rstd[:, 0:n], bank[6][:, 0:n], ACT.Sqrt, bias=small[:, 7:8], scale=1.0 / D).then_inc(S("n_sqrt"), 1)

            def norm_hi(m, n, col, between=None):
                for g in range(4):
                    if between and g == 2:
                        between()
                    act.wait_ge(S("n_xn"), 4 * m + g + 1)
                    for c in range(4):
                        ins = act.activation(hh[:, 4 * g + c, 0:n], nb[:, g % 2, c, 0:n], ACT.Copy,
                                             scale=gains[:, col, 4 * g + c:4 * g + c + 1])
                    ins.then_inc(S("n_hi"), 1)

            act.sem_inc(S("g_o"), 1)
            for name in ("st_out0", "st_out1", "stp_out"):
                act.sem_inc(S(name), 16)
            act.wait_ge(S("params_in"), PARAMS)
            for g in range(4):
                act.wait_ge(S(f"first_x{g}"), 16)
                if g >= 2:
                    act.wait_ge(S("n_ss"), g - 1)
                act.activation(nb[:, g % 2, :, :], x_res[:, 4 * g:4 * g + 4, :], ACT.Square).then_inc(S("n_sq"), 1)
            act.activation(n_hi[:, :], n_raw[:, :], ACT.Copy).then_inc(S("nw_hi"), 1)
            cast(0, 0, 0, C)
            norm_root(0, T)
            cast(0, 0, 1, C)
            norm_hi(0, T, 0)
            act.wait_ge(S("lf_neg"), 1)
            ch.link(act.activation(lf_t[:, 1, :], lf_t[:, 1, :], ACT.Exp))
            act.activation(lf_t[:, 1, :], lf_t[:, 1, :], ACT.Ln, bias=ones[0:ND, 0:1]).then_inc(S("lf_ln"), 1)

            def fox_step(i, k, b):
                step("fox", i, k, b)

            def q_copy(t):
                act.wait_ge(S("q_ps"), t + 1)
                if not (isinstance(t, int) and t == 0):
                    act.wait_ge(S("k_used"), 16 * t)
                for n in range(2):
                    ins = act.activation(qb[:, 512 * n:512 * n + 512], bank[2 + n][:, :], ACT.Copy, scale=SCALE)
                ins.then_inc(S("q_b"), 1)

            some_panels(act, 0, 2, fox_step)
            act.wait_ge(S("gg_neg"), 1)
            ch.link(act.activation(g_t[:, 1, :, :], g_t[:, 1, :, :], ACT.Exp))
            act.activation(g_t[:, 1, :, :], g_t[:, 1, :, :], ACT.Ln, bias=ones[:, 0:1]).then_inc(S("gg_ln"), 1)
            act.wait_ge(S("gates_done"), 1)
            act.activation(g_eg, g_log[:, :, NP_:T], ACT.Exp).then_inc(S("g_eg"), 1)
            for i in range(2, 6):
                for k in range(4):
                    fox_step(i, k, C)
                    if (i, k) == (2, 0):
                        q_copy(0)
                if i == 2:
                    act.wait_ge(S("t_ps"), 1)
                    for n in range(2):
                        ins = act.activation(t_sb[:, 512 * n:512 * n + 512], bank[2 + n][:, :], ACT.Copy)
                    ins.then_inc(S("t_sb"), 1)
            act.wait_ge(S("z_fox"), 1)
            act.dma_start(io["o_kv"], flat(z[:, 8:24, :])).then_inc(S("out_act"), 16)
            act.dma_start(io["o_logf"], logf[:, :]).then_inc(S("out_act"), 16)

            def exp_scores(t):
                act.wait_ge(S("s_sub"), t)
                act.activation(prob[:, :, 0:H], s_bias, ACT.Exp)
                act.activation(sm8[:, 16:24], sm8[:, 16:24], ACT.Exp).then_inc(S("p_ready"), 1)

            def take_o(t):
                act.wait_ge(S("v_used"), 16 * t)
                act.activation(osb[:, :], bank[4][:, 0:256], ACT.Copy).then_inc(S("o_sb"), 1)

            def panel_turn(t, name, i0, more=None):
                for k in range(8):
                    if k == 2:
                        exp_scores(t)
                    if k == 7:
                        take_o(t)
                    step(name, i0 + k // 4, k % 4, C)
                    if more:
                        more(k)
                q_copy(t + 1)

            def memory_squares(k):
                for g in {1: (0, 1), 5: (2, 3)}.get(k, ()):
                    act.wait_ge(S(f"nb_in{g % 2}"), 16 * (g // 2 + 1))
                    act.activation(nb[:, g % 2, :, 0:MEM], nb[:, g % 2, :, 0:MEM], ACT.Square).then_inc(S("n_sq"), 1)
                if k == 7:
                    norm_root(1, MEM)

            q_copy(1)
            panel_turn(1, "gla", 0, memory_squares)
            with act.Fori(2, 4) as t:
                panel_turn(t, "gla", 2 * t - 2)
            norm_hi(1, MEM, 2, between=lambda: exp_scores(4))
            for k in range(8):
                if k == 7:
                    take_o(4)
                step("mem", k // 4, k % 4, C if k < 6 else 0)
            q_copy(5)
            act.wait_ge(S("mkv_done"), 1)
            act.dma_start(io["o_mkv"], flat(mkv)).then_inc(S("out_act"), 16)
            act.activation(z[:, 40:48, :], z[:, 40:48, :], ACT.Silu)

            def f_stage(n, qsrc, vsrc):
                a_q, a_v, a_vn, _, _, _, _, vbank = a_set(n)
                wait_apart(act, "a_free", n + 1)
                act.activation(a_q[:, :], qsrc, ACT.Copy, scale=SCALE)
                act.activation(a_v[:, :], vsrc, ACT.Copy).then_inc(S("a_staged"), 1)
                act.wait_ge(S("a_vps"), n + 1)
                act.activation(flat(a_vn), vbank[:, 0:256], ACT.Copy).then_inc(S("a_vn"), 1)

            def f_exp(n):
                _, _, _, a_s, _, m, _, _ = a_set(n)
                act.wait_ge(S("a_max"), n + 1)
                for q in range(2):
                    ins = act.activation(a_s[:, q, :], a_s[:, q, :], ACT.Exp, bias=sm8[:, m + 2 + q:m + 3 + q],
                                         accum_out=sm8[:, m + 4 + q:m + 5 + q])
                ins.then_inc(S("a_exp"), 1)

            def f_scale(n):
                _, _, _, a_s, _, m, _, _ = a_set(n)
                act.wait_ge(S("a_rec"), n + 1)
                for q in range(2):
                    ins = act.activation(a_s[:, q, :], a_s[:, q, :], ACT.Copy, scale=sm8[:, m + 6 + q:m + 7 + q])
                ins.then_inc(S("a_p"), 1)

            def f_pt(n):
                _, _, _, _, a_pt, _, sbank, _ = a_set(n)
                act.wait_ge(S("a_ptps"), n + 1)
                act.activation(flat(a_pt), sbank[:, :], ACT.Copy).then_inc(S("a_pt"), 1)

            def f_out_hi(n, i):
                wait_apart(act, "a_ops", n + 1)
                act.activation(hh[:, ds(i, 1), 0:NP_], row(a_set(n)[-1][:, 0:256]), ACT.Copy).then_inc(S("a_ohi"), 1)

            s_in = io["s0"].rearrange("(b h k) v -> b k h v", h=GH, k=P)
            s_out = io["o_sts"].rearrange("(b h k) v -> b k h v", h=GH, k=P)

            def state_load(i, s):
                act.wait_ge(S("gs_free"), 2 * i + s + 1)
                act.wait_ge(S(f"st_out{s}"), 16 * i + 16)
                act.dma_start(g_s[:, s, :].rearrange("p (h v) -> p h v", h=GH),
                              s_in[ds(2 * i + s, 1), :, :, :].rearrange("a k h v -> k (a h) v")).then_inc(S(f"st_in{s}"), 16)

            def state_decay(i, s):
                act.wait_ge(S("gd_cols"), 2 * i + s + 1)
                act.wait_ge(S(f"st_in{s}"), 16 * (i + 1))
                for h in range(GH):
                    ins = act.activation(g_s[:, s, 256 * h:256 * h + 256], g_s[:, s, 256 * h:256 * h + 256], ACT.Copy,
                                         scale=g_cols[:, s, 2, h:h + 1])
                ins.then_inc(S("gd_dec"), 1)

            def state_store(i, s):
                act.wait_ge(S("gd_new"), 2 * i + s + 1)
                act.dma_start(s_out[ds(2 * i + s, 1), :, :, :].rearrange("a k h v -> k (a h) v"),
                              g_s[:, s, :].rearrange("p (h v) -> p h v", h=GH)).then_inc(S(f"st_out{s}"), 16)

            def head_turn(t, i):
                def fox_args(c):
                    return flat(z[:, ds(2 * i + c, 1), 0:NP_]), flat(z[:, ds(2 * H + 2 * i + c, 1), 0:NP_])
                for s in range(2):
                    state_load(i, s)
                state_decay(i, 0)
                exp_scores(t)
                f_stage(2 * i, *fox_args(0))
                wait_apart(act, "g_free", i + 1)
                act.activation(g_q, flat(z[:, ds(24 + i, 1), 0:NP_]), ACT.Copy, scale=SCALE)
                act.activation(g_k, flat(z[:, ds(28 + i, 1), 0:NP_]), ACT.Copy)
                act.activation(g_v, z[:, ds(32 + 2 * i, 2), 0:NP_], ACT.Copy).then_inc(S("g_staged"), 1)
                act.wait_ge(S("g_diff"), i + 1)
                act.activation(g_d[:, 0:LEVELS, :], g_d[:, 0:LEVELS, :], ACT.Abs).then_inc(S("g_abs"), 1)
                act.activation(g_eb, g_b, ACT.Exp)
                act.activation(g_d[:, LEVELS, :], g_d[:, LEVELS, :], ACT.Exp)
                act.wait_ge(S("g_abs"), i + 1)
                act.activation(g_d[:, 0:LEVELS, :], g_d[:, 0:LEVELS, :], ACT.Exp, scale=-1.0).then_inc(S("g_exp"), 1)
                act.wait_ge(S("g_vps"), i + 1)
                act.activation(flat(g_vn), bank[0][:, :], ACT.Copy).then_inc(S("g_vn"), 1)
                f_exp(2 * i)
                state_store(i, 0)
                state_decay(i, 1)
                f_scale(2 * i)
                act.wait_ge(S("g_kps"), i + 1)
                act.activation(flat(g_kn), bank[1][:, 0:256], ACT.Copy).then_inc(S("g_kn"), 1)
                f_pt(2 * i)
                state_store(i, 1)
                f_out_hi(2 * i, 2 * i)
                f_stage(2 * i + 1, *fox_args(1))
                act.wait_ge(S("g_state"), i + 1)
                act.dma_start(io["o_stp"][ds(i * P, P), :], g_st[:, 3, :]).then_inc(S("stp_out"), 16)
                wait_apart(act, "g_ops", i + 1)
                act.activation(z[:, ds(32 + 2 * i, 2), 0:NP_], bank[0][:, :].rearrange("p (a b) -> p a b", a=2), ACT.Copy
                               ).then_inc(S("g_o"), 1)
                f_exp(2 * i + 1)
                f_scale(2 * i + 1)
                f_pt(2 * i + 1)
                take_o(t)
                f_out_hi(2 * i + 1, 2 * i + 1)
                if not (isinstance(t, int) and t >= 7):
                    q_copy(t + 1)

            with act.Fori(5, 7) as t:
                head_turn(t, t - 5)
            head_turn(7, 2)
            head_turn(8, 3)
            act.wait_ge(S("ofd_all"), 1)
            act.activation(hh[:, 0:H, NP_:T], ofd, ACT.Copy).then_inc(S("ofd_hi"), 1)

            act.wait_ge(S("hn_go"), 1)
            for h in range(GH):
                act.activation(g_sq[:, 2 * h:2 * h + 2, :], z[:, 32 + 2 * h:34 + 2 * h, :], ACT.Square).then_inc(S("hn_sq"), 1)
            for h in range(GH):
                act.wait_ge(S("hn_ss"), h + 1)
                act.activation(g_rs[:, h, :], bank[HN_BANKS[h]][:, 0:T], ACT.Sqrt, bias=small[:, 7:8], scale=1.0 / DV
                               ).then_inc(S("hn_sqrt"), 1)
            cast(ST["out"][0], 0, 0, C)
            cast(ST["out"][0], 0, 1, C)
            for h in range(GH):
                act.wait_ge(S("hn_out"), h + 1)
                act.activation(hh[:, 8 + 2 * h:10 + 2 * h, :], z[:, 32 + 2 * h:34 + 2 * h, :], ACT.Copy).then_inc(S("hn_hi"), 1)

            casts("out")
            norm_root(2, T)
            norm_hi(2, T, 1)
            casts("xq")
            def x_query(b):
                act.wait_ge(S("xq_ps"), b + 1)
                if b >= 2:
                    act.wait_ge(S("xk_used"), b - 1)
                act.activation(x_qb[:, b % 2, :], bank[2 + b % 2][:, :], ACT.Copy, scale=SCALE).then_inc(S("xq_b"), 1)

            def x_take(b):
                act.wait_ge(S("xv_used"), b + 1)
                if b >= 2:
                    act.wait_ge(S("xo_ps"), b - 1)
                act.activation(x_o[:, P * (b % 2):P * (b % 2) + P], x_bank(b)[:, 0:P], ACT.Copy).then_inc(S("xo_sb"), 1)

            def x_stage(i):
                f_stage(H + i, x_q[:, i, 0:NP_], mkv[:, XH + i, :])

            x_stage(0)
            x_stage(1)
            x_query(0)
            x_query(1)
            f_exp(H)
            f_exp(H + 1)
            x_query(2)
            x_query(3)
            f_scale(H)
            f_scale(H + 1)
            f_pt(H)
            f_pt(H + 1)
            x_query(4)
            x_query(5)
            f_out_hi(H, 0)
            x_query(6)
            x_query(7)
            f_out_hi(H + 1, 1)
            x_stage(2)
            x_stage(3)
            f_exp(H + 2)
            f_exp(H + 3)
            act.wait_ge(S("x_sub"), 1)
            act.activation(x_p[:, :, :, 0:XH], x_s, ACT.Exp).then_inc(S("x_exp"), 1)
            f_scale(H + 2)
            f_scale(H + 3)
            f_pt(H + 2)
            f_pt(H + 3)
            x_take(0)
            x_take(1)
            f_out_hi(H + 2, 2)
            x_take(2)
            x_take(3)
            f_out_hi(H + 3, 3)
            for b in range(4, ND):
                x_take(b)
            act.wait_ge(S("xod_ready"), 1)
            act.activation(hh[:, 0:XH, NP_:T], x_od, ACT.Copy).then_inc(S("xod_hi"), 1)
            casts("xo")
            norm_root(3, T)
            norm_hi(3, T, 3)

            def gate_up(half):
                name, (first, count, _) = f"gu{half}", ST[f"gu{half}"]

                def gu_step(i, k, blocks):
                    c = k // 2
                    chunk = HALF * half + 2 * i + c
                    if k == 0:
                        act.activation(sm8[:, 62:63], ones[:, 0:1], ACT.Silu)
                    if k % 2 == 0:
                        step(name, i, k, blocks)
                        act.wait_ge(S("h_mul"), chunk + 1)
                        act.activation(f_sg[:, :], bank[0][:, 0:T], ACT.Silu).then_inc(S("acc0_free"), 1)
                    else:
                        step(name, i, k, blocks)
                        wait_apart(act, "h_mul", chunk + 2)
                        act.activation(f_hi[:, ds(2 * i + c, 1), :], row(f_h[:, c, :]), ACT.Copy).then_inc(S("h_hi"), 1)
                for_panels(act, ch, name, gu_step)

            for half in range(2):
                gate_up(half)
                casts(f"dn{half}")
            norm_root(4, T)
            act.wait_ge(S("out_act"), 48)
            act.wait_ge(S("stp_out"), 16 * GH + 16)

        @block.vector
        def _(dve):
            ch = Chain(dve, "dve_chain")
            tt, ts, stt = dve.tensor_tensor, dve.tensor_scalar, dve.scalar_tensor_tensor

            def split(first, i, k, blocks):
                dve.wait_ge(S("w_hi"), first + 4 * i + k + 1)
                tt(wlo[:, k % 4, 0:blocks * P], raw[:, k % 4, 0:blocks * P], whi[:, k % 2, 0:blocks * P], ALU.subtract
                   ).then_inc(S("w_split"), 1)

            def step(name, i, k, blocks, evac):
                first = ST[name][0]
                dve.wait_ge(S("mm_done"), first + 4 * i + k + 1)
                evac(i, k)
                if blocks:
                    split(first, i, k + 2, blocks)

            def panels(name, evac):
                for_panels(dve, ch, name, lambda i, k, b: step(name, i, k, b, evac))

            def to_z(tile0):
                return lambda i, k: dve.tensor_copy(z[:, ds(tile0 + 4 * i + k, 1), :], row(bank[k % 2][:, 0:T])
                                                    ).then_inc(S(f"acc{k % 2}_free"), 1)

            def add_x(i, k):
                xs = x_res[:, ds(4 * i + k, 1), :]
                tt(xs, row(bank[k % 2][:, 0:T]), xs, ALU.add).then_inc(S(f"acc{k % 2}_free"), 1)

            def own(sem, value):
                dve.wait_ge(S(sem), value)

            def norm(m, n, col, streamed, final=False, between=None):
                r = rstd[:, 0:n]
                if not streamed:
                    ch.link(dve.tensor_copy(sm8[:, 60:61], ones[:, 0:1]))
                dve.wait_ge(S("n_sqrt"), m + 1)
                ch.link(dve.reciprocal(r, r))
                rb = row(r).broadcast_to([P, 4, n])

                def lo(g):
                    dve.wait_ge(S("n_hi"), 4 * m + g + 1)
                    for c in range(4):
                        ins = stt(hl[:, 4 * g + c, 0:n], nb[:, g % 2, c, 0:n], gains[:, col, 4 * g + c:4 * g + c + 1],
                                  hh[:, 4 * g + c, 0:n], ALU.mult, ALU.subtract)
                    ins.then_inc(S("n_lo_done"), 1)

                for g in range(4):
                    if final:
                        for c in range(4 * g, 4 * g + 4):
                            ins = stt(x_res[:, c, :], x_res[:, c, :], gains[:, col, c:c + 1], r, ALU.mult, ALU.mult)
                        ins.then_inc(S("y_done"), 1)
                        continue
                    cur = nb[:, g % 2, :, 0:n]
                    if streamed:
                        dve.wait_ge(S(f"nb_in{g % 2}"), 16 * (2 + g // 2 + 1))
                    if g >= 2:
                        own("n_lo_done", 4 * m + g - 1)
                    tt(cur, cur if streamed else x_res[:, 4 * g:4 * g + 4, :], rb, ALU.mult).then_inc(S("n_xn"), 1)
                    if between:
                        between(g)
                    if g:
                        lo(g - 1)
                if not final:
                    lo(3)
                    own("n_lo_done", 4 * m + 4)

            for name in ("acc0_free", "acc1_free", "h_mul"):
                dve.sem_inc(S(name), 1)
            dve.wait_ge(S("nw_hi"), 1)
            tt(n_lo[:, :], n_raw[:, :], n_hi[:, :], ALU.subtract).then_inc(S("nw_lo"), 1)
            split(0, 0, 0, C)
            norm(0, T, 0, False)
            split(0, 0, 1, C)
            dve.memset(prob, 0.0)
            dve.wait_ge(S("nw_ps"), 1)
            ch.link(dve.tensor_copy(ggs[:, :], bank[7][0:RANK, 0:T]))
            u, ex = lf_t[:, 0, :], lf_t[:, 1, :]
            ch.link(ts(u, bank[7][32:32 + ND, 0:T], small[0:ND, 6:7], None, ALU.add))
            stt(ex, u, -1.0, u, ALU.mult, ALU.min).then_inc(S("lf_neg"), 1)
            dve.wait_ge(S("lf_ln"), 1)
            ch.link(stt(logf[:, :], u, 0.0, ex, ALU.min, ALU.subtract))
            ch.link(dve.tensor_tensor_scan(ndq[:, :], ones[0:ND, 0:1].broadcast_to([ND, NP_]), logf[:, 0:NP_], 0.0,
                                           ALU.mult, ALU.add))
            ch.link(ts(ndq[:, :], ndq[:, :], -1.0, None, ALU.mult))
            ch.link(tt(lf_in, colv(ident[0:ND, 0:H]).broadcast_to([ND, H, ND]), row(logf[:, NP_:T]).broadcast_to([ND, H, ND]), ALU.mult))
            dve.sem_inc(S("ds_in"), 1)

            def q_diag(t):
                tt(qd[:, :].rearrange("p (a b) -> p a b", a=H), row(ident).broadcast_to([P, H, P]),
                   z[:, 0:H, ds(NP_ + t, 1)].broadcast_to([P, H, P]), ALU.mult).then_inc(S("q_diag"), 1)

            tail4 = tail[:, :].rearrange("p (h b j) -> p j b h", h=H, b=ND)

            def k_page(t, j):
                q = j if isinstance(t, int) and t == 0 else MIX.index(("k", j))
                slot = q % SLOTS
                dve.wait_ge(S(f"page_in{slot}"), arrived(t, q))
                for h in range(H):
                    pk = page[:, slot, P * h:P * h + P]
                    ins = dve.tensor_tensor_reduce(out=pk, in0=pk, in1=qb[:, P * h:P * h + P], scale=1.0, scalar=0.0,
                                                   op0=ALU.mult, op1=ALU.add, accum_out=s_raw[:, j, h:h + 1])
                ins.then_inc(S("k_used"), 1)

            def s_max(t):
                own("k_used", 16 * t + 16)
                ch.link(tt(s_bias.rearrange("p (j b) h -> p j b h", b=1), s_raw.rearrange("p (j b) h -> p j b h", b=1),
                           tail4[:, :, ds(t, 1), :], ALU.add))
                ch.link(dve.tensor_reduce(sm8[:, 0:H], s_bias.rearrange("p j h -> p h j"), AX.X, ALU.max))
                tt(colv(sm8[:, 0:H]), colv(sm8[:, 0:H]), snew[:, :, ds(t, 1)], ALU.max).then_inc(S("mx_ready"), 1)

            def sm_diag(t):
                dve.wait_ge(S("mx_ps"), t)
                ch.link(dve.tensor_reduce(sm8[0:H, 40:41], bank[5][0:H, 0:P], AX.X, ALU.max))
                ts(sm8[0:H, 32:40], ident[0:H, 0:H], sm8[0:H, 40:41], None, ALU.mult).then_inc(S("m_diag"), 1)

            def sm_sub(t):
                dve.wait_ge(S("m_ps"), t)
                mb = bank[5][:, 128:136]
                ch.link(tt(s_bias, s_bias, row(mb).broadcast_to([P, PAGES, H]), ALU.subtract))
                tt(colv(sm8[:, 16:24]), snew[:, :, ds(t - 1, 1)], colv(mb), ALU.subtract).then_inc(S("s_sub"), 1)

            def sm_sum(t):
                dve.wait_ge(S("p_ready"), t)
                dve.tensor_reduce(sm8[:, 8:16], prob[:, :, 0:H].rearrange("p j h -> p h j"), AX.X, ALU.add
                                  ).then_inc(S("l_part"), 1)

            def sm_rec(t):
                dve.wait_ge(S("l_ps"), t)
                tt(sm8[:, 24:32], sm8[:, 16:24], bank[5][:, 136:144], ALU.add).then_inc(S("l_read"), 1)
                own("l_read", t)
                ch.link(dve.reciprocal(sm8[:, 24:32], sm8[:, 24:32]))

            def sm_out(t):
                dve.wait_ge(S("o_ps"), t)
                t8 = colv(sm8[:, 16:24])
                ch.link(tt(t8, t8, z[:, 2 * H:3 * H, ds(NP_ - 1 + t, 1)], ALU.mult))
                t42 = sm8[:, 16:24].rearrange("p (g e) -> p g e", e=2)
                ch.link(tt(t42, t42, bank[5][:, 144:152].rearrange("p (e g) -> p g e", e=2), ALU.add))
                ch.link(tt(ofd[:, :, ds(t - 1, 1)], t8, colv(sm8[:, 24:32]), ALU.mult))

            def fox_step(i, k, b):
                step("fox", i, k, b, to_z(0))

            some_panels(dve, 0, 2, fox_step)
            dve.wait_ge(S("gg_ps"), 1)
            for c in range(GH):
                ins = ts(g_t[:, 0, c, :], bank[2 + c][:, 0:T], small[:, 2 + c:3 + c], None, ALU.add)
            ch.link(ins)
            gu, ge = flat(g_t[:, 0, :, :]), flat(g_t[:, 1, :, :])
            stt(ge, gu, -1.0, gu, ALU.mult, ALU.min).then_inc(S("gg_neg"), 1)
            q_diag(0)
            dve.wait_ge(S("gg_ln"), 1)
            ch.link(stt(flat(g_t[:, 2, :, :]), gu, 0.0, ge, ALU.min, ALU.subtract))
            ts(flat(g_log), flat(g_t[:, 2, :, :]), 1.0 / 16.0, None, ALU.mult).then_inc(S("gates_done"), 1)
            for i in range(2, 6):
                for k in range(4):
                    fox_step(i, k, C)
                    if (i, k) == (2, 0):
                        dve.wait_ge(S("q_b"), 1)
                    if (i, k) == (3, 1):
                        dve.wait_ge(S("t_ps"), 1)
                        for n in range(2):
                            dve.tensor_copy(r_sb[:, 512 * n:512 * n + 512], bank[6 + n][:, :])
                        dve.tensor_copy(lfb, bank[5][:, 0:64].rearrange("p (a b) -> p a b", a=H)).then_inc(S("r_sb"), 1)
                        own("r_sb", 1)
                    if (i, k) == (4, 0):
                        ch.link(dve.tensor_copy(sm8[:, 60:61], ones[:, 0:1]))
                        tt(sq_in, z[:, 0:H, NP_:T], z[:, H:2 * H, NP_:T], ALU.mult).then_inc(S("sq_in"), 1)
                    if (i, k) == (4, 1):
                        dve.wait_ge(S("tail_ps"), 1)
                        for n in range(2):
                            ch.link(tt(tail[:, 512 * n:512 * n + 512].rearrange("p (a j) -> p a j", j=PAGES),
                                       bank[2 + n][:, :].rearrange("p (a j) -> p a j", j=PAGES),
                                       colv(flat(lfb)[:, 32 * n:32 * n + 32]).broadcast_to([P, 32, PAGES]), ALU.add))
                    if (i, k) == (5, 1):
                        dve.wait_ge(S("sq_ps"), 1)
                        ch.link(ts(snew, bank[5][:, 64:128].rearrange("p (a b) -> p a b", a=H), SCALE, None, ALU.mult))
                        dve.sem_inc(S("tail_ready"), 1)
                    k_page(0, 4 * i + k - 8)
            ch.link(dve.tensor_copy(sm8[:, 60:61], ones[:, 0:1]))
            dve.sem_inc(S("z_fox"), 1)
            s_max(0)
            q_diag(1)
            dve.wait_ge(S("g_eg"), 1)

            def panel_turn(t, evac, name, i0):
                dve.wait_ge(S("q_b"), t + 1)
                for k, piece in enumerate((sm_diag, sm_sub, sm_sum, sm_rec, None, None, None, None)):
                    k_page(t, 2 * k)
                    k_page(t, 2 * k + 1)
                    step(name, i0 + k // 4, k % 4, C, evac)
                    if piece:
                        piece(t)
                    if k == 3:
                        q_diag(t + 1)
                sm_out(t)
                s_max(t)

            LINKS = 8
            panel_turn(1, to_z(24), "gla", 0)
            first = ch.count
            with dve.Fori(2, 4) as t:
                ch.turn(first, t - 2, LINKS)
                panel_turn(t, to_z(24), "gla", 2 * t - 2)
            ch.after(first, 2, LINKS)
            dve.wait_ge(S("q_b"), 5)

            def between(g):
                k_page(4, 2 * g)
                k_page(4, 2 * g + 1)
                (sm_diag, sm_sub, sm_sum, sm_rec)[g](4)
            norm(1, MEM, 2, True, between=between)
            for k in range(8):
                k_page(4, 8 + k)
                step("mem", k // 4, k % 4, C if k < 6 else 0,
                     lambda i, k: dve.tensor_copy(mkv[:, 4 * i + k, :], bank[k % 2][:, 0:MEM]).then_inc(S(f"acc{k % 2}_free"), 1))
                if k == 3:
                    q_diag(5)
            sm_out(4)
            s_max(4)
            dve.sem_inc(S("mkv_done"), 1)
            ch.link(dve.memset(g_at, 0.0))
            for _ in range(2):
                dve.sem_inc(S("gs_free"), 1)

            def f_start(i, causal_):
                if causal_:
                    tt(row(a_nd[:, :]), row(ndq[:, :]), row(ident[0:ND, ds(i, 1)]).broadcast_to([ND, 1, NP_]), ALU.mult)
                    ch.link(dve.memset(A_SETS[0][3][:, 0, P:256], -1e30))
                dve.sem_inc(S("a_free"), 1)

            def f_max(n, causal_):
                _, _, _, a_s, _, m, sbank, _ = a_set(n)
                dve.wait_ge(S("a_sc"), n + 1)
                if causal_:
                    tt(a_s[:, 0, 0:P], sbank[:, 0:P], causal, ALU.add)
                    dve.tensor_copy(a_s[:, 1, 0:P], sbank[:, 256:384])
                    ch.link(tt(a_s[:, 1, P:256], sbank[:, 384:512], causal, ALU.add))
                else:
                    ch.link(dve.tensor_copy(flat(a_s), sbank[:, :]))
                ch.link(dve.tensor_reduce(sm8[:, m:m + 2], a_s, AX.X, ALU.max))
                ts(sm8[:, m + 2:m + 4], sm8[:, m:m + 2], -1.0, None, ALU.mult).then_inc(S("a_max"), 1)

            def f_rec(n):
                m = a_set(n)[5]
                dve.wait_ge(S("a_exp"), n + 1)
                dve.reciprocal(sm8[:, m + 6:m + 8], sm8[:, m + 4:m + 6]).then_inc(S("a_rec"), 1)

            def f_out_lo(n, i):
                dve.wait_ge(S("a_ohi"), n + 1)
                ch.link(tt(hl[:, ds(i, 1), 0:NP_], row(a_set(n)[-1][:, 0:256]), hh[:, ds(i, 1), 0:NP_], ALU.subtract))

            def gd_start(b, s):
                dve.tensor_copy(colv(g_cols[:, s, 0, :]), z[:, 28:32, ds(NP_ + b, 1)])
                ts(colv(g_cols[:, s, 1, :]), z[:, 24:28, ds(NP_ + b, 1)], SCALE, None, ALU.mult)
                ch.link(dve.tensor_copy(colv(g_cols[:, s, 2, :]), g_eg[:, :, ds(b, 1)]))
                dve.sem_inc(S("gd_cols"), 1)
                tt(g_dd[:, :].rearrange("p (a b) -> p a b", a=8), row(ident).broadcast_to([P, 8, P]),
                   z[:, 32:40, ds(NP_ + b, 1)].broadcast_to([P, 8, P]), ALU.mult).then_inc(S("gd_diag"), 1)

            def gd_update(b, s):
                dve.wait_ge(S("gd_v"), b + 1)
                dve.wait_ge(S("gd_dec"), b + 1)
                for h in range(GH):
                    st = g_s[:, s, 256 * h:256 * h + 256]
                    ins = stt(st, bank[2 + h // 2][:, 256 * (h % 2):256 * (h % 2) + 256], g_cols[:, s, 0, h:h + 1], st, ALU.mult, ALU.add)
                ins.then_inc(S("gd_new"), 1)

            def gd_out(b):
                dve.wait_ge(S("gd_o"), b + 1)
                ch.link(dve.tensor_copy(g_ofd[:, :, ds(b, 1)], colv(bank[2][:, 0:8])))
                dve.sem_inc(S("gs_free"), 1)

            def g_diffs(i):
                dve.wait_ge(S("g_o"), i + 1)
                dve.sem_inc(S("g_free"), 1)
                ch.link(dve.tensor_tensor_scan(g_b, kst[:, K_SCAN:K_SCAN + NP_], flat(g_log[:, ds(i, 1), 0:NP_]), 0.0,
                                               ALU.mult, ALU.add))
                for l in range(LEVELS):
                    n, half = 256 >> (l + 1), 1 << l
                    b2 = g_b.rearrange("p (n c) -> p n c", c=2 * half)
                    tt(g_d[:, l, :].rearrange("p (n c) -> p n c", c=2 * half), b2,
                       b2[:, :, half - 1:half].broadcast_to([P, n, 2 * half]), ALU.subtract)
                b4 = g_b.rearrange("p (n c) -> p n c", c=64)
                tt(g_d[:, LEVELS, :].rearrange("p (n c) -> p n c", c=64), b4[:, :, 63:64].broadcast_to([P, 4, 64]), b4, ALU.subtract
                   ).then_inc(S("g_diff"), 1)

            def g_products(i):
                dve.wait_ge(S("g_exp"), i + 1)
                for l in range(LEVELS):
                    half = 1 << l
                    kq = bass.AP(tensor=g_kq.tensor, offset=0, ap=[[512, P], [2 * half, 128 >> l], [256 + half, 2], [1, half]])
                    d = g_d[:, l, :].rearrange("p (n two c) -> p n two c", two=2, c=half)
                    tt(d, d, kq, ALU.mult)
                tt(g_ke, g_d[:, LEVELS, :], g_k, ALU.mult)
                tt(g_qe, g_q, g_eb, ALU.mult).then_inc(S("g_qk"), 1)

            def g_levels(i, lo, hi):
                for l in range(lo, hi):
                    dve.wait_ge(S("g_aps"), (LEVELS + 1) * i + l + 1)
                    dve.tensor_copy(sm8[:, 60:61], ones[:, 0:1])
                    mask = masks[:, l * P:(l + 1) * P]
                    dve.copy_predicated(g_at, row(mask).broadcast_to([P, 2, P]), bank[l % 2][:, 0:256].rearrange("p (a b) -> p a b", a=2)
                                        ).then_inc(S("g_cp"), 1)
                    own("g_cp", (LEVELS + 1) * i + l + 1)

            def g_states(i):
                dve.wait_ge(S("g_kv"), i + 1)
                dve.wait_ge(S("stp_out"), 16 * i + 16)
                kv = [bank[c % 2][:, 256 * (c // 2):256 * (c // 2) + 256] for c in range(4)]
                ch.link(dve.tensor_copy(g_st[:, 0, :], kv[0]))
                for c in range(1, 4):
                    ch.link(stt(g_st[:, c, :], g_st[:, c - 1, :], g_eb[:, 64 * c + 63:64 * c + 64], kv[c], ALU.mult, ALU.add))
                dve.sem_inc(S("g_state"), 1)

            def head_turn(t, i):
                more = not (isinstance(t, int) and t == 8)

                def piece(j):
                    if j == 0:
                        sm_diag(t)
                        gd_start(2 * i, 0)
                    elif j == 1:
                        sm_sub(t)
                        f_start(2 * i, True)
                    elif j == 2:
                        g_diffs(i)
                    elif j == 3:
                        sm_sum(t)
                        gd_update(2 * i, 0)
                    elif j == 4:
                        sm_rec(t)
                        f_max(2 * i, True)
                    elif j == 5:
                        g_products(i)
                        gd_out(2 * i)
                        gd_start(2 * i + 1, 1)
                    elif j == 6:
                        f_rec(2 * i)
                    elif j == 7:
                        gd_update(2 * i + 1, 1)
                    elif j == 8:
                        g_levels(i, 0, 2)
                    elif j == 9:
                        gd_out(2 * i + 1)
                        if more and not (isinstance(t, int) and t == 7):
                            q_diag(t + 1)
                        g_levels(i, 2, 4)
                    elif j == 10:
                        f_out_lo(2 * i, 2 * i)
                        g_levels(i, 4, LEVELS + 1)
                    elif j == 11:
                        f_start(2 * i + 1, True)
                    elif j == 12:
                        g_states(i)
                    elif j == 13:
                        f_max(2 * i + 1, True)
                    elif j == 14:
                        f_rec(2 * i + 1)
                    else:
                        sm_out(t)
                        if more:
                            s_max(t)
                        f_out_lo(2 * i + 1, 2 * i + 1)

                if more:
                    dve.wait_ge(S("q_b"), t + 1)
                for j in range(PAGES):
                    if more:
                        k_page(t, j)
                    piece(j)

            HLINKS = 25
            first = ch.count
            with dve.Fori(5, 7) as t:
                ch.turn(first, t - 5, HLINKS)
                head_turn(t, t - 5)
            ch.after(first, 2, HLINKS)
            head_turn(7, 2)
            head_turn(8, 3)
            dve.sem_inc(S("ofd_all"), 1)
            dve.wait_ge(S("ofd_hi"), 1)
            ch.link(tt(hl[:, 0:H, NP_:T], ofd, hh[:, 0:H, NP_:T], ALU.subtract))
            dve.wait_ge(S("g_o"), GH + 1)

            dve.wait_ge(S("stp_out"), 16 * GH + 16)
            for s in range(2):
                dve.wait_ge(S(f"st_out{s}"), 16 * ND // 2 + 16)
            dve.sem_inc(S("ring_free"), 1)
            ch.link(dve.tensor_copy(z[:, 32:40, NP_:T], g_ofd))
            dve.sem_inc(S("hn_go"), 1)
            for h in range(GH):
                dve.wait_ge(S("hn_sqrt"), h + 1)
                ch.link(dve.reciprocal(g_rs[:, h, :], g_rs[:, h, :]))
                o2 = z[:, 32 + 2 * h:34 + 2 * h, :]
                ch.link(tt(o2, o2, row(g_rs[:, h, :]).broadcast_to([P, 2, T]), ALU.mult))
                for j in range(2):
                    oj = z[:, 32 + 2 * h + j, :]
                    ins = stt(oj, oj, small[:, j:j + 1], z[:, 40 + 2 * h + j, :], ALU.mult, ALU.mult)
                ins.then_inc(S("hn_out"), 1)
                if h == 1:
                    split(ST["out"][0], 0, 0, C)
            for h in range(GH):
                dve.wait_ge(S("hn_hi"), h + 1)
                ins = tt(hl[:, 8 + 2 * h:10 + 2 * h, :], z[:, 32 + 2 * h:34 + 2 * h, :], hh[:, 8 + 2 * h:10 + 2 * h, :], ALU.subtract)
            ch.link(ins)
            dve.wait_ge(S("out_act"), 48)
            dve.sem_inc(S("gla_done"), 1)
            split(ST["out"][0], 0, 1, C)
            dve.wait_ge(S("x_in"), 16)
            panels("out", add_x)
            norm(2, T, 1, False)
            panels("xq", lambda i, k: dve.tensor_copy(x_q[:, k, :], bank[k % 2][:, 0:T]).then_inc(S(f"acc{k % 2}_free"), 1))
            ch.link(dve.memset(x_p, 0.0))
            def x_diag(b):
                if b:
                    dve.wait_ge(S("xq_ps"), b)
                tt(x_qd[:, :].rearrange("p (a b) -> p a b", a=XH), row(ident).broadcast_to([P, XH, P]),
                   x_q[:, :, NP_ + b:NP_ + b + 1].broadcast_to([P, XH, P]), ALU.mult).then_inc(S("xq_diag"), 1)

            def x_scores(b):
                dve.wait_ge(S("xq_b"), b + 1)
                dve.wait_ge(S(f"page_in{b}"), 16 * 33)
                for m in range(2):
                    for h in range(XH):
                        pk = page[:, b, 512 * m + P * h:512 * m + P * h + P]
                        ins = dve.tensor_tensor_reduce(out=pk, in0=pk, in1=x_qb[:, b % 2, P * h:P * h + P], scale=1.0, scalar=0.0,
                                                       op0=ALU.mult, op1=ALU.add, accum_out=x_s[:, b, m, h:h + 1])
                ins.then_inc(S("xk_used"), 1)

            f_start(0, False)
            f_start(1, False)
            x_diag(0)
            f_max(H, False)
            x_diag(1)
            f_max(H + 1, False)
            x_scores(0)
            x_diag(2)
            x_scores(1)
            x_diag(3)
            f_rec(H)
            f_rec(H + 1)
            x_scores(2)
            x_diag(4)
            x_scores(3)
            x_diag(5)
            x_scores(4)
            x_diag(6)
            x_scores(5)
            x_diag(7)
            f_out_lo(H, 0)
            x_scores(6)
            x_scores(7)
            f_out_lo(H + 1, 1)
            f_start(2, False)
            f_start(3, False)
            own("xk_used", ND)
            bh = "p (b h) -> p b h"
            tt(x_sm[:, 0:32].rearrange(bh, b=ND), x_s[:, :, 0, :], x_s[:, :, 1, :], ALU.max).then_inc(S("xmx_ready"), 1)
            f_max(H + 2, False)
            dve.wait_ge(S("xmx_ps"), 1)
            ch.link(dve.tensor_reduce(x_sm[0:32, 64:65], bank[5][0:32, 0:P], AX.X, ALU.max))
            ts(x_sm[0:32, 96:128], ident[0:32, 0:32], x_sm[0:32, 64:65], None, ALU.mult).then_inc(S("xm_diag"), 1)
            f_max(H + 3, False)
            dve.wait_ge(S("xm_ps"), 1)
            mb = bank[5][:, P:P + 32].rearrange(bh, b=ND)
            for m in range(2):
                ins = tt(x_s[:, :, m, :], x_s[:, :, m, :], mb, ALU.subtract)
            ins.then_inc(S("x_sub"), 1)
            f_rec(H + 2)
            f_rec(H + 3)
            dve.wait_ge(S("x_exp"), 1)
            tt(x_sm[:, 32:64].rearrange(bh, b=ND), x_p[:, :, 0, 0:XH], x_p[:, :, 1, 0:XH], ALU.add).then_inc(S("xl_part"), 1)
            dve.wait_ge(S("xl_ps"), 1)
            dve.reciprocal(x_sm[:, 128:160], bank[5][:, 160:192]).then_inc(S("xl_read"), 1)
            own("xl_read", 1)
            f_out_lo(H + 2, 2)
            f_out_lo(H + 3, 3)
            dve.wait_ge(S("xo_ps"), ND)
            tt(x_od.rearrange("p h b -> p b h"), bank[5][:, 192:224].rearrange(bh, b=ND), x_sm[:, 128:160].rearrange(bh, b=ND), ALU.mult
               ).then_inc(S("xod_ready"), 1)
            dve.wait_ge(S("xod_hi"), 1)
            ch.link(tt(hl[:, 0:XH, NP_:T], x_od, hh[:, 0:XH, NP_:T], ALU.subtract))
            dve.sem_inc(S("xo_go"), 1)


            def xo_step(i, k, blocks):
                first = ST["xo"][0]
                for j in range(4):
                    if j < 3:
                        dve.wait_ge(S("xo_tile"), 3 * k + j + 1)
                    else:
                        dve.wait_ge(S("mm_done"), first + k + 1)
                    xs = x_res[:, 4 * k + j, :]
                    tt(xs, bank[j % 2][:, 0:T], xs, ALU.add).then_inc(S(f"acc{j % 2}_free"), 1)
                split(first, 0, k + 2, blocks)

            for_panels(dve, ch, "xo", xo_step)
            norm(3, T, 3, False)

            def gate_up(half):
                name, (first, _, _) = f"gu{half}", ST[f"gu{half}"]

                def gu_step(i, k, blocks):
                    c = k // 2
                    chunk = HALF * half + 2 * i + c
                    dve.wait_ge(S("mm_done"), first + 4 * i + k + 1)
                    if k % 2 == 1:
                        dve.wait_ge(S("acc0_free"), (ACC[name] // 2) + 2 * i + c + 2)
                        tt(f_h[:, c, :], bank[1][:, 0:T], f_sg[:, :], ALU.mult).then_inc(S("h_mul"), 1)
                        own("h_mul", chunk + 2)
                        dve.sem_inc(S("acc1_free"), 1)
                    split(first, i, k + 2, blocks)
                    if k % 2 == 1:
                        dve.wait_ge(S("h_hi"), chunk + 1)
                        tt(f_lo[:, ds(2 * i + c, 1), :], row(f_h[:, c, :]), f_hi[:, ds(2 * i + c, 1), :], ALU.subtract).then_inc(S("h_lo"), 1)
                for_panels(dve, ch, name, gu_step)

            def add_down(i, k):
                if k % 2 == 1:
                    xs = x_res[:, ds(2 * i + k // 2, 1), :]
                    tt(xs, row(bank[k // 2][:, 0:T]), xs, ALU.add).then_inc(S(f"acc{k // 2}_free"), 1)

            for half in range(2):
                gate_up(half)
                panels(f"dn{half}", add_down)
            norm(4, T, 4, False, final=True)

        @block.tensor
        def _(pe):
            mm = pe.matmul
            NORMED = {"mem": 1, "xq": 2, "gu0": 3}

            def blk(t, slot, b):
                return t[:, slot, P * b:P * b + P]

            def three(out, k, b, rh, rl, start, stop):
                mm(out, blk(whi, k % 2, b), rh, start=start, stop=False)
                mm(out, blk(whi, k % 2, b), rl, start=False, stop=False)
                return mm(out, blk(wlo, k, b), rh, start=False, stop=stop)

            def panel(name, i, k, n=T):
                first, _, blocks = ST[name]
                pe.wait_ge(S("w_split"), first + 4 * i + k + 1)
                pe.wait_ge(S(f"acc{k % 2}_free"), ACC[name] // 2 + 2 * i + k // 2 + 1)
                for b in range(blocks):
                    if k == 0 and b == 8 and name == "out":
                        pe.wait_ge(S("gla_done"), 1)
                    if k == 0 and b % 4 == 0 and name in NORMED:
                        pe.wait_ge(S("n_lo_done"), 4 * NORMED[name] + b // 4 + 1)
                    last = three(bank[k % 2][:, 0:n], k, b, hh[:, b, 0:n], hl[:, b, 0:n], b == 0, b == blocks - 1)
                last.then_inc(S("mm_done"), 1)

            def panels(name, n=T):
                with pe.Fori(0, ST[name][1] // 4) as i:
                    for k in range(4):
                        panel(name, i, k, n)

            def norm(m, n, lo=0, hi=4):
                for g in range(lo, hi):
                    pe.wait_ge(S("n_sq"), 4 * m + g + 1)
                    for c in range(4):
                        last = mm(bank[6][:, 0:n], ones, nb[:, g % 2, c, 0:n], start=(g == 0 and c == 0), stop=(g == 3 and c == 3))
                    last.then_inc(S("n_ss"), 1)

            def norm_sum(m):
                pe.wait_ge(S("n_acc"), m - 1)
                mm(bank[6][:, 0:T], ones, s_acc[:, :], start=True, stop=True).then_inc(S("n_ss"), 4)

            pe.wait_ge(S("params_in"), PARAMS)
            norm(0, T)
            pe.wait_ge(S("nw_lo"), 1)
            for b in range(C):
                if b % 4 == 0:
                    pe.wait_ge(S("n_lo_done"), b // 4 + 1)
                w = slice(NARROW * b, NARROW * b + NARROW)
                mm(bank[7][0:NARROW, 0:T], n_hi[:, w], hh[:, b, :], start=b == 0, stop=False)
                mm(bank[7][0:NARROW, 0:T], n_hi[:, w], hl[:, b, :], start=False, stop=False)
                last = mm(bank[7][0:NARROW, 0:T], n_lo[:, w], hh[:, b, :], start=False, stop=b == C - 1)
            last.then_inc(S("nw_ps"), 1)

            def q_spread(t):
                pe.wait_ge(S("q_diag"), t + 1)
                for n in range(2):
                    last = mm(bank[2 + n][:, :], ones, qd[:, 512 * n:512 * n + 512], start=True, stop=True)
                last.then_inc(S("q_ps"), 1)

            def fox(i, k, b=None):
                panel("fox", i, k)

            some_panels(pe, 0, 2, fox)
            for c in range(GH):
                last = mm(bank[2 + c][:, 0:T], wgate[:, P * c:P * c + P], ggs[:, :], start=True, stop=True)
            last.then_inc(S("gg_ps"), 1)
            for i in range(2, 6):
                for k in range(4):
                    fox(i, k)
                    if (i, k) == (2, 0):
                        q_spread(0)
                if i == 2:
                    pe.wait_ge(S("lf_in"), 16)
                    pe.wait_ge(S("ds_in"), 1)
                    pe.wait_ge(S("q_b"), 1)
                    fk = f_nat[:, :].rearrange("p (k h) -> p h k", h=H)
                    for h in range(H):
                        mm(bank[2 + h // 4][:, P * (h % 4):P * (h % 4) + P], fk[:, h, :], ident, start=True, stop=True)
                        mm(bank[6 + h // 4][:, P * (h % 4):P * (h % 4) + P], fk[:, h, :], later[:, P:2 * P], start=True, stop=True)
                    mm(bank[5][:, 0:64], ones[0:ND, :], flat(lf_in), start=True, stop=True).then_inc(S("t_ps"), 1)
                elif i == 3:
                    pe.wait_ge(S("t_sb"), 1)
                    pe.wait_ge(S("r_sb"), 1)
                    for n in range(2):
                        mm(bank[2 + n][:, :], later[:, 0:P], t_sb[:, 512 * n:512 * n + 512], start=True, stop=False)
                        last = mm(bank[2 + n][:, :], ones, r_sb[:, 512 * n:512 * n + 512], start=False, stop=True)
                    last.then_inc(S("tail_ps"), 1)
                elif i == 4:
                    pe.wait_ge(S("sq_in"), 1)
                    mm(bank[5][:, 64:128], ones, flat(sq_in), start=True, stop=True).then_inc(S("sq_ps"), 1)
            def sm_mx(t):
                pe.wait_ge(S("mx_ready"), t)
                pe.transpose(bank[5][0:H, 0:P], sm8[:, 0:H], ident).then_inc(S("mx_ps"), 1)

            def sm_m(t):
                pe.wait_ge(S("m_diag"), t)
                mm(bank[5][:, 128:136], ones[0:H, :], sm8[0:H, 32:40], start=True, stop=True).then_inc(S("m_ps"), 1)

            def sm_l(t):
                pe.wait_ge(S("l_part"), t)
                mm(bank[5][:, 136:144], ones, sm8[:, 8:16], start=True, stop=True).then_inc(S("l_ps"), 1)

            def pv(t, lo, hi):
                for j in range(lo, hi):
                    q = MIX.index(("v", j)) if not (isinstance(t, int) and t == 8) else j
                    pe.wait_ge(S(f"page_in{q % SLOTS}"), arrived(t, q))
                    for g in range(4):
                        last = mm(bank[4][32 * g:32 * g + 32, 0:256], prob[:, j, :], page[:, q % SLOTS, 256 * g:256 * g + 256],
                                  start=j == 0, stop=j == PAGES - 1)
                    last.then_inc(S("v_used"), 1)

            def extract(t):
                pe.wait_ge(S("o_sb"), t)
                pe.wait_ge(S("l_read"), t)
                for e in range(2):
                    last = mm(bank[5][:, 144 + 4 * e:148 + 4 * e], osb[:, P * e:P * e + P], kst[:, K_SEL + 4 * e:K_SEL + 4 * e + 4],
                              start=True, stop=True)
                last.then_inc(S("o_ps"), 1)

            def panel_turn(t, name, i0, n):
                first = isinstance(t, int)

                def one(k):
                    panel(name, i0 + k // 4, k % 4, n)
                one(0)
                if first:
                    q_spread(t)
                sm_mx(t)
                one(1)
                sm_m(t)
                one(2)
                if first:
                    norm(1, MEM, 0, 2)
                one(3)
                sm_l(t)
                pv(t, 0, 2)
                one(4)
                q_spread(t + 1)
                pv(t, 2, 6)
                one(5)
                pv(t, 6, 11)
                one(6)
                if first:
                    norm(1, MEM, 2, 4)
                pv(t, 11, 16)
                one(7)
                extract(t)

            panel_turn(1, "gla", 0, T)
            with pe.Fori(2, 4) as t:
                panel_turn(t, "gla", 2 * t - 2, T)
            sm_mx(4)
            sm_m(4)
            sm_l(4)
            pv(4, 0, 4)
            for k in range(8):
                panel("mem", k // 4, k % 4, MEM)
                pv(4, min(4 + 2 * k, PAGES), min(6 + 2 * k, PAGES))
                if k == 5:
                    q_spread(5)
            extract(4)

            def f_scores(n, kap, causal_):
                a_q, a_v, _, _, _, _, sbank, vbank = a_set(n)
                pe.wait_ge(S("a_staged"), n + 1)
                for q in range(2):
                    last = pe.transpose(vbank[:, P * q:P * q + P], a_v[:, P * q:P * q + P], ident)
                last.then_inc(S("a_vps"), 1)
                if causal_:
                    for q in range(2):
                        w = P * (q + 1)
                        mm(sbank[:, 256 * q:256 * q + w], a_q[:, P * q:P * q + P], kap(w), start=True, stop=False)
                        last = mm(sbank[:, 256 * q:256 * q + w], ones[0:ND, :], a_nd[:, 0:w], start=False, stop=True)
                else:
                    for q in range(2):
                        last = mm(sbank[:, 256 * q:256 * q + 256], a_q[:, P * q:P * q + P], kap(256), start=True, stop=True)
                last.then_inc(S("a_sc"), 1)

            def f_turned(n):
                _, _, _, a_s, _, _, sbank, _ = a_set(n)
                pe.wait_ge(S("a_p"), n + 1)
                for kt in range(2):
                    for q in range(2):
                        last = pe.transpose(sbank[:, 256 * kt + P * q:256 * kt + P * q + P], a_s[:, q, P * kt:P * kt + P], ident)
                last.then_inc(S("a_ptps"), 1)

            def f_out(n):
                _, _, a_vn, _, a_pt, _, _, vbank = a_set(n)
                pe.wait_ge(S("a_vn"), n + 1)
                pe.wait_ge(S("a_pt"), n + 1)
                mm(vbank[:, 0:256], a_vn[:, 0, :], a_pt[:, 0, :], start=True, stop=False)
                mm(vbank[:, 0:256], a_vn[:, 1, :], a_pt[:, 1, :], start=False, stop=True).then_inc(S("a_ops"), 1)

            def gd_spread(b):
                pe.wait_ge(S("gd_diag"), b + 1)
                for n in range(2):
                    last = mm(bank[2 + n][:, :], ones, g_dd[:, 512 * n:512 * n + 512], start=True, stop=True)
                last.then_inc(S("gd_v"), 1)

            def gd_query(b, s):
                pe.wait_ge(S("gd_new"), b + 1)
                for h in range(GH):
                    for j in range(2):
                        last = mm(bank[2][:, 2 * h + j:2 * h + j + 1], g_s[:, s, 256 * h + P * j:256 * h + P * j + P],
                                  g_cols[:, s, 1, h:h + 1], start=True, stop=True)
                last.then_inc(S("gd_o"), 1)

            def g_turn_v(i):
                pe.wait_ge(S("g_staged"), i + 1)
                for t in range(2):
                    for j in range(2):
                        last = pe.transpose(bank[0][:, 256 * t + P * j:256 * t + P * j + P], g_v[:, j, P * t:P * t + P], ident)
                last.then_inc(S("g_vps"), 1)

            def g_turn_k(i):
                pe.wait_ge(S("g_qk"), i + 1)
                for t in range(2):
                    last = pe.transpose(bank[1][:, P * t:P * t + P], g_ke[:, P * t:P * t + P], ident)
                last.then_inc(S("g_kps"), 1)

            def g_level(i, l):
                if l < 2:
                    pe.wait_ge(S(("g_vn", "g_kn")[l]), i + 1)
                else:
                    pe.wait_ge(S("g_cp"), (LEVELS + 1) * i + l - 1)
                k, q = (g_d[:, l, :], g_d[:, l, :]) if l < LEVELS else (g_k, g_q)
                for t in range(2):
                    last = mm(bank[l % 2][:, P * t:P * t + P], k[:, P * t:P * t + P], q[:, P * t:P * t + P], start=True, stop=True)
                last.then_inc(S("g_aps"), 1)

            def g_kv(i):
                pe.wait_ge(S("g_cp"), (LEVELS + 1) * (i + 1))
                for c in range(4):
                    r = slice(64 * (c % 2), 64 * (c % 2) + 64)
                    last = mm(bank[c % 2][:, 256 * (c // 2):256 * (c // 2) + 256], g_kn[r, c // 2, :], g_vn[r, c // 2, :],
                              start=True, stop=True)
                last.then_inc(S("g_kv"), 1)

            def g_out(i):
                pe.wait_ge(S("g_state"), i + 1)
                for j in range(2):
                    for t in range(2):
                        mm(bank[0][:, 256 * j + P * t:256 * j + P * t + P], g_vn[:, t, P * j:P * j + P], g_at[:, t, :],
                           start=t == 0, stop=False, skip_group_check=True)
                    for c in range(1, 4):
                        last = mm(bank[0][:, 256 * j + 64 * c:256 * j + 64 * c + 64], g_st[:, c - 1, P * j:P * j + P],
                                  g_qe[:, 64 * c:64 * c + 64], start=False, stop=c == 3, skip_group_check=True)
                last.then_inc(S("g_ops"), 1)

            def head_turn(t, i):
                def kap(c):
                    return lambda w: flat(z[:, ds(H + 2 * i + c, 1), 0:w])
                sm_mx(t)
                sm_m(t)
                gd_spread(2 * i)
                f_scores(2 * i, kap(0), True)
                g_turn_v(i)
                sm_l(t)
                gd_query(2 * i, 0)
                gd_spread(2 * i + 1)
                g_turn_k(i)
                g_level(i, 0)
                f_turned(2 * i)
                g_level(i, 1)
                gd_query(2 * i + 1, 1)
                f_out(2 * i)
                pv(t, 0, 2)
                g_level(i, 2)
                g_level(i, 3)
                pv(t, 2, 4)
                if not (isinstance(t, int) and t >= 7):
                    q_spread(t + 1)
                g_level(i, 4)
                g_level(i, 5)
                pv(t, 4, 6)
                g_level(i, 6)
                g_kv(i)
                pv(t, 6, 8)
                f_scores(2 * i + 1, kap(1), True)
                pv(t, 8, 10)
                g_out(i)
                pv(t, 10, 14)
                f_turned(2 * i + 1)
                pv(t, 14, 16)
                f_out(2 * i + 1)
                extract(t)

            with pe.Fori(5, 7) as t:
                head_turn(t, t - 5)
            head_turn(7, 2)
            head_turn(8, 3)
            for h in range(GH):
                pe.wait_ge(S("hn_sq"), h + 1)
                mm(bank[HN_BANKS[h]][:, 0:T], ones, g_sq[:, 2 * h, :], start=True, stop=False)
                mm(bank[HN_BANKS[h]][:, 0:T], ones, g_sq[:, 2 * h + 1, :], start=False, stop=True).then_inc(S("hn_ss"), 1)

            panels("out")
            norm_sum(2)
            panels("xq")
            def x_spread(b):
                pe.wait_ge(S("xq_diag"), b + 1)
                if b >= 2:
                    pe.wait_ge(S("xq_b"), b - 1)
                mm(bank[2 + b % 2][:, :], ones, x_qd[:, :], start=True, stop=True).then_inc(S("xq_ps"), 1)

            def x_pv(b):
                pe.wait_ge(S(f"page_in{b}"), 16 * 34)
                if b >= 2:
                    pe.wait_ge(S("xo_sb"), b - 1)
                else:
                    pe.wait_ge(S("x_exp"), 1)
                for m in range(2):
                    for g in range(4):
                        last = mm(x_bank(b)[32 * g:32 * g + 32, 0:P], x_p[:, b, m, :],
                                  page[:, b, 512 * m + P * g:512 * m + P * g + P], start=m == 0, stop=m == 1)
                last.then_inc(S("xv_used"), 1)

            def x_extract(b):
                pe.wait_ge(S("xo_sb"), b + 1)
                mm(bank[5][:, 192 + 4 * b:196 + 4 * b], x_o[:, P * (b % 2):P * (b % 2) + P], kst[:, K_SEL + 8:K_SEL + 12],
                   start=True, stop=True).then_inc(S("xo_ps"), 1)

            def x_head(i):
                f_scores(H + i, lambda w: mkv[:, i, 0:w], False)

            x_head(0)
            x_head(1)
            for b in range(4):
                x_spread(b)
            f_turned(H)
            f_turned(H + 1)
            x_spread(4)
            x_spread(5)
            f_out(H)
            x_spread(6)
            x_spread(7)
            f_out(H + 1)
            x_head(2)
            x_head(3)
            pe.wait_ge(S("xmx_ready"), 1)
            pe.transpose(bank[5][0:32, 0:P], x_sm[:, 0:32], ident).then_inc(S("xmx_ps"), 1)
            pe.wait_ge(S("xm_diag"), 1)
            mm(bank[5][:, P:P + 32], ones[0:32, :], x_sm[0:32, 96:128], start=True, stop=True).then_inc(S("xm_ps"), 1)
            f_turned(H + 2)
            f_turned(H + 3)
            pe.wait_ge(S("xl_part"), 1)
            mm(bank[5][:, 160:192], ones, x_sm[:, 32:64], start=True, stop=True).then_inc(S("xl_ps"), 1)
            x_pv(0)
            x_pv(1)
            f_out(H + 2)
            pe.wait_ge(S("xl_read"), 1)
            x_extract(0)
            x_pv(2)
            x_extract(1)
            x_pv(3)
            f_out(H + 3)
            for b in range(4, ND + 2):
                x_extract(b - 2)
                if b < ND:
                    x_pv(b)
            pe.wait_ge(S("xo_go"), 1)
            for k in range(ST["xo"][1]):
                pe.wait_ge(S("w_split"), ST["xo"][0] + k + 1)
                for j in range(4):
                    pe.wait_ge(S(f"acc{j % 2}_free"), ACC["xo"] // 2 + 2 * k + j // 2 + 1)
                    for b in range(XH):
                        last = three(bank[j % 2][:, 0:T], k, XH * j + b, hh[:, b, :], hl[:, b, :], b == 0, b == XH - 1)
                    last.then_inc(S("xo_tile" if j < 3 else "mm_done"), 1)
            norm_sum(3)
            for half in range(2):
                panels(f"gu{half}")
                name = f"dn{half}"
                first = ST[name][0]
                pe.wait_ge(S("h_lo"), HALF * (half + 1))
                with pe.Fori(0, 8) as i:
                    for k in range(4):
                        pe.wait_ge(S("w_split"), first + 4 * i + k + 1)
                        if k % 2 == 0:
                            pe.wait_ge(S(f"acc{k // 2}_free"), ACC[name] // 2 + i + 1)
                        for b in range(SUB):
                            kk = SUB * (k % 2) + b
                            last = three(bank[k // 2][:, 0:T], k, b, f_hi[:, kk, :], f_lo[:, kk, :], kk == 0, kk == HALF - 1)
                        last.then_inc(S("mm_done"), 1)
            norm_sum(4)


def panels_of(w):
    k, n = w.shape
    return np.ascontiguousarray(w.reshape(k // P, P, n // P, P).transpose(2, 1, 0, 3).reshape(n, k))


def chunks_of(a):
    return np.ascontiguousarray(a.T.reshape(-1, P, a.shape[0]).transpose(1, 0, 2).reshape(P, -1))


def kernel(**x):
    import concourse.bacc as bacc
    from concourse.bass_utils import run_bass_kernel_spmd

    x = {n: np.asarray(a) for n, a in x.items()}
    w_in = x["w_in"][0]
    splits = np.cumsum((1024, 1024, 1024, 8, 512, 512, 1024, 1024, 16))
    narrow = np.zeros((D, NARROW), np.float32)
    narrow[:, 0:RANK] = w_in[:, splits[7]:splits[8]]
    narrow[:, 32:40] = w_in[:, splits[2]:splits[3]]
    gate, up = panels_of(x["w_ffn_gate"][0]), panels_of(x["w_ffn_up"][0])
    gu = np.stack([gate.reshape(-1, P, D), up.reshape(-1, P, D)], 1).reshape(-1, D)
    down = x["w_ffn_down"][0].reshape(2, 2, SUB, P, C, P).transpose(0, 4, 1, 3, 2, 5).reshape(-1, SUB * P)
    kst, later, masks = constants()
    small = np.zeros((P, 8), np.float32)
    small[:, 0:2] = x["g_gla_head"][0].reshape(2, P).T
    small[:, 2:6] = x["b_gla_gate"][0].reshape(4, P).T
    small[0:H, 6] = x["b_forget"][0]
    small[:, 7] = EPS
    n_pool = x["cache_fox_k"].shape[1]
    ins = {
        "x_fm": chunks_of(np.concatenate([x["x_prompt"][0], x["x_sample"][:, 0]])),
        "mem_fm": chunks_of(x["mem_prompt"][0]),
        "gains": np.concatenate([g.reshape(C, P).T for g in (x["g_mix"], x["g_cross"], x["g_mem"], x["g_ffn"], x["g_final"])], 1),
        "kst": kst, "masks": masks, "later": later, "small": small, "wgate": x["w_gla_gate"][0],
        "w_narrow": narrow.reshape(C, P, NARROW).transpose(1, 0, 2).reshape(P, -1),
        "p_fox": panels_of(w_in[:, 0:splits[2]]), "p_gla": panels_of(w_in[:, splits[3]:splits[7]]),
        "p_mem": np.concatenate([panels_of(x["w_xk"][0]), panels_of(x["w_xv"][0])]),
        "p_out": panels_of(x["w_out"][0]), "p_xq": panels_of(x["w_xq"][0]), "p_xo": panels_of(x["w_xo"][0]).reshape(4, 4, P, XH * P).transpose(0, 2, 1, 3).reshape(4 * P, C * P),
        "p_gu0": gu[0:len(gu) // 2], "p_gu1": gu[len(gu) // 2:], "p_dn0": down[0:len(down) // 2], "p_dn1": down[len(down) // 2:],
        "kc": x["cache_fox_k"].reshape(n_pool * PAGE, H * P), "vc": x["cache_fox_v"].reshape(n_pool * PAGE, H * P),
        "lf": x["cache_fox_logf"].reshape(n_pool, PAGE * H),
        "pt_row": x["page_table"].reshape(1, -1), "pt_col": x["page_table"].reshape(-1, 1),
        "s0": x["state_gla"].reshape(-1, DV), "cmk": x["cache_mem_k"].reshape(-1, XH * P), "cmv": x["cache_mem_v"].reshape(-1, XH * P),
    }
    outs = {"o_y": (P, C * T), "o_kv": (P, 2 * H * T), "o_logf": (ND, T), "o_stp": (GH * P, DV), "o_mkv": (P, 2 * XH * MEM),
            "o_sts": (ND * GH * P, DV)}
    nc = bacc.Bacc("TRN2", target_bir_lowering=False, num_devices=1)
    arrays, io = {}, {"n_pool": n_pool}
    for name, a in ins.items():
        arrays[name + "_dram"] = np.ascontiguousarray(a)
        io[name] = nc.dram_tensor(name + "_dram", a.shape, mybir.dt.from_np(a.dtype), kind="ExternalInput").ap()
    for name, shape in outs.items():
        io[name] = nc.dram_tensor(name + "_dram", shape, mybir.dt.float32, kind="ExternalOutput").ap()
    build(nc, io)
    r = run_bass_kernel_spmd(nc, [arrays], core_ids=[0]).results[0]
    r = {name: np.asarray(r[name + "_dram"]) for name in outs}

    y = r["o_y"].reshape(P, C, T).transpose(2, 1, 0).reshape(T, D)
    kv = r["o_kv"].reshape(P, 2, H, T).transpose(1, 3, 2, 0)
    lf = r["o_logf"].T
    mkv = r["o_mkv"].reshape(P, 2, XH, MEM).transpose(1, 3, 2, 0)
    c = np.ascontiguousarray
    return (c(y[0:NP_])[None], c(y[NP_:])[:, None],
            c(kv[0, 0:NP_])[None, None], c(kv[1, 0:NP_])[None, None], c(lf[0:NP_])[None, None],
            r["o_stp"].reshape(1, 1, GH, P, DV), c(mkv[0])[None, None], c(mkv[1])[None, None],
            c(kv[0, NP_:])[None, :, None], c(kv[1, NP_:])[None, :, None], c(lf[NP_:])[None, :, None],
            r["o_sts"].reshape(1, ND, GH, P, DV))
```
